# Optimizing a Trainium2 kernel written in Bass

```python
import jax, jax.numpy as jnp
from jax import lax
import numpy as np

D_MODEL = 1024
BATCH = 1
SEQ = 256
DEPTH = 2
DEC_BATCH = 8
DEC_SEQ = 4
PAST_LEN = 2048
PAGE_SIZE = 128

N_AB_LAYERS = (DEPTH + 1) // 2
N_C_LAYERS = DEPTH // 2
H_A = 8
N_A = 64
C_A = H_A * N_A
W_LORA = 64
A_LORA = 64
G_LORA = 128
A_SHIFT_COLS = 3 * C_A + W_LORA + A_LORA + G_LORA
RWKV_GN_EPS = 64e-5
H_B = 4
DK_B = 128
DV_B = 128
C_B = H_B * DV_B
RET_CHUNK = 128
ROPE_THETA = 10000.0
RET_GN_EPS = 1e-5
AB_COLS = A_SHIFT_COLS + 2 * H_B * DK_B + 2 * C_B
H_C = 8
DK_C = 128
DV_C = 128
C_C = H_C * DV_C
CONV_W = 4
GDN_CHUNK = 64
N_QKV_C = 2 * H_C * DK_C + C_C
C_COLS = N_QKV_C + 2 * H_C + C_C
D_FF = 2816
LN_EPS = 1e-5
DEEPNORM_ALPHA = (2 * DEPTH) ** 0.25
DEEPNORM_BETA = (8 * DEPTH) ** -0.25

kernel_name = 'rwkv7_retnet_gdn_macaron_deepnorm_step'

def layer_norm(x, g, b):
    xf = x.astype(jnp.float32)
    xc = xf - jnp.mean(xf, -1, keepdims=True)
    var = jnp.mean(xc * xc, -1, keepdims=True)
    return xc * lax.rsqrt(var + LN_EPS) * g + b

def group_norm(x, g, b, eps):
    xf = x.astype(jnp.float32)
    xc = xf - jnp.mean(xf, -1, keepdims=True)
    var = jnp.mean(xc * xc, -1, keepdims=True)
    shp = x.shape[-2:]
    return xc * lax.rsqrt(var + eps) * g.reshape(shp) + b.reshape(shp)

def l2_normalize(x):
    xf = x.astype(jnp.float32)
    return xf * lax.rsqrt(jnp.maximum(jnp.sum(xf * xf, -1, keepdims=True), 1e-12))

def swiglu(x, wg, wu, wd):
    return (jax.nn.silu(x @ wg) * (x @ wu)) @ wd

def rotary(x, pos):
    half = x.shape[-1] // 2
    inv_freq = 1.0 / (ROPE_THETA ** jnp.linspace(0.0, 1.0, half, dtype=jnp.float32))
    ang = pos[:, None] * inv_freq[None, :]
    cos = jnp.cos(ang)[None, :, None, :]
    sin = jnp.sin(ang)[None, :, None, :]
    x1, x2 = x[..., :half], x[..., half:]
    return jnp.concatenate([x1 * cos - x2 * sin, x2 * cos + x1 * sin], -1)

def retention_log_gamma():
    return jnp.log(1.0 - jnp.exp2(-5.0 - jnp.arange(H_B, dtype=jnp.float32)))

def rwkv7_recurrence(r, decay, k, v, kk, a, S0):
    def step(S, inp):
        r_t, w_t, k_t, v_t, kk_t, a_t = inp
        sk = jnp.einsum('bhvk,bhk->bhv', S, kk_t)
        S = (S * w_t[:, :, None, :] - sk[..., None] * (kk_t * a_t)[:, :, None, :]
             + v_t[..., None] * k_t[:, :, None, :])
        return S, jnp.einsum('bhvk,bhk->bhv', S, r_t)
    xs = tuple(jnp.moveaxis(t.astype(jnp.float32), 1, 0) for t in (r, decay, k, v, kk, a))
    S, o = lax.scan(step, S0.astype(jnp.float32), xs)
    return jnp.moveaxis(o, 0, 1), S

def retention_chunked(q, k, v, S0):
    Bn, L, H, DK = q.shape
    DV = v.shape[-1]
    C = RET_CHUNK if L % RET_CHUNK == 0 else L
    n = L // C
    blk = lambda t: t.astype(jnp.float32).reshape(Bn, n, C, H, t.shape[-1]).transpose(1, 0, 3, 2, 4)
    q, k, v = blk(q), blk(k), blk(v)
    lg = retention_log_gamma()
    idx = jnp.arange(C, dtype=jnp.float32)
    rel = idx[:, None] - idx[None, :]
    causal = rel >= 0
    dmat = jnp.where(causal, jnp.exp(jnp.where(causal, rel, 0.0)[None] * lg[:, None, None]), 0.0)
    xi = jnp.exp((idx[None, :] + 1.0) * lg[:, None])[..., None]
    zeta = jnp.exp((C - 1.0 - idx[None, :]) * lg[:, None])[..., None]
    g_chunk = jnp.exp(C * lg)[:, None, None]
    inner = (jnp.einsum('nbhid,nbhjd->nbhij', q, k) * dmat) @ v
    kz = k * zeta

    def step(S, inp):
        q_c, kz_c, v_c = inp
        o = (q_c @ S) * xi
        S = g_chunk * S + jnp.swapaxes(kz_c, -1, -2) @ v_c
        return S, o
    S, cross = lax.scan(step, S0.astype(jnp.float32), (q, kz, v))
    o = (inner + cross).transpose(1, 0, 3, 2, 4).reshape(Bn, L, H, DV)
    return o, S

def gated_delta_chunked(q, k, v, g, beta, S0):
    Bn, L, H, DK = q.shape
    DV = v.shape[-1]
    C = GDN_CHUNK if L % GDN_CHUNK == 0 else L
    n = L // C
    blk4 = lambda t: t.astype(jnp.float32).reshape(Bn, n, C, H, t.shape[-1]).transpose(1, 0, 3, 2, 4)
    blk3 = lambda t: t.astype(jnp.float32).reshape(Bn, n, C, H).transpose(1, 0, 3, 2)
    q = blk4(q) * DK ** -0.5
    k, v = blk4(k), blk4(v)
    g, beta = blk3(g), blk3(beta)
    gc = jnp.cumsum(g, -1)
    idx = jnp.arange(C)
    incl = idx[:, None] >= idx[None, :]
    strict = idx[:, None] > idx[None, :]
    diff = gc[..., :, None] - gc[..., None, :]
    dmat = jnp.where(incl, jnp.exp(jnp.where(incl, diff, 0.0)), 0.0)
    kb = k * beta[..., None]
    A = jnp.where(strict, jnp.einsum('nbhid,nbhjd->nbhij', kb, k) * dmat, 0.0)
    eye = jnp.eye(C, dtype=jnp.float32)
    T = lax.linalg.triangular_solve(A + eye, jnp.broadcast_to(eye, A.shape),
                                    left_side=True, lower=True, unit_diagonal=True)
    u = T @ (v * beta[..., None])
    w = T @ (kb * jnp.exp(gc)[..., None])
    qk = jnp.einsum('nbhid,nbhjd->nbhij', q, k) * dmat
    qg = q * jnp.exp(gc)[..., None]
    kd = k * jnp.exp(gc[..., -1:] - gc)[..., None]
    g_last = jnp.exp(gc[..., -1])[..., None, None]

    def step(S, inp):
        u_c, w_c, qk_c, qg_c, kd_c, gl_c = inp
        v_new = u_c - w_c @ S
        o = qg_c @ S + qk_c @ v_new
        S = gl_c * S + jnp.swapaxes(kd_c, -1, -2) @ v_new
        return S, o
    S, o = lax.scan(step, S0.astype(jnp.float32), (u, w, qk, qg, kd, g_last))
    return o.transpose(1, 0, 3, 2, 4).reshape(Bn, L, H, DV), S

def ab_mixer(h, pos, shift_prev, S_rwkv0, S_ret0, p, i):
    Bn, L, _ = h.shape
    z = (h @ p['ab_w_in'][i]).astype(jnp.float32)
    za, zb = z[..., :A_SHIFT_COLS], z[..., A_SHIFT_COLS:]
    za_prev = jnp.concatenate([shift_prev.astype(jnp.float32)[:, None, :], za[:, :-1]], axis=1)
    zs = za + (za_prev - za) * p['rwkv_mu'][i]
    r, k, v, wd, ad, gd = jnp.split(
        zs, (C_A, 2 * C_A, 3 * C_A, 3 * C_A + W_LORA, 3 * C_A + W_LORA + A_LORA), axis=-1)
    w_log = -jax.nn.softplus(-(p['rwkv_w0'][i] + jnp.tanh(wd) @ p['rwkv_w2'][i])) - 0.5
    decay = jnp.exp(-jnp.exp(w_log))
    a = jax.nn.sigmoid(p['rwkv_a0'][i] + ad @ p['rwkv_a2'][i])
    gate = jax.nn.sigmoid(gd) @ p['rwkv_g2'][i]
    split_a = lambda t: t.reshape(Bn, L, H_A, N_A)
    kk = l2_normalize(split_a(k * p['rwkv_k_k'][i]))
    k = k * (1.0 + (a - 1.0) * p['rwkv_k_a'][i])
    r_h, k_h, v_h, a_h = split_a(r), split_a(k), split_a(v), split_a(a)
    o_a, S_rwkv = rwkv7_recurrence(r_h, split_a(decay), k_h, v_h, kk, a_h, S_rwkv0)
    o_a = (group_norm(o_a, p['rwkv_gn_g'][i], p['rwkv_gn_b'][i], RWKV_GN_EPS)
           + jnp.sum(r_h * k_h * p['rwkv_r_k'][i], -1, keepdims=True) * v_h)
    o_a = o_a.reshape(Bn, L, C_A) * gate
    qr, kr, vr, gr = jnp.split(zb, (H_B * DK_B, 2 * H_B * DK_B, 2 * H_B * DK_B + C_B), axis=-1)
    qr = rotary(qr.reshape(Bn, L, H_B, DK_B), pos)
    kr = rotary(kr.reshape(Bn, L, H_B, DK_B), pos) * DK_B ** -0.5
    o_b, S_ret = retention_chunked(qr, kr, vr.reshape(Bn, L, H_B, DV_B), S_ret0)
    o_b = group_norm(o_b, p['ret_gn_g'][i], p['ret_gn_b'][i], RET_GN_EPS).reshape(Bn, L, C_B) * jax.nn.silu(gr)
    out = jnp.concatenate([o_a, o_b], -1) @ p['ab_w_out'][i]
    return out, za[:, -1], S_rwkv, S_ret

def gdn_mixer(h, conv_prev, S0, p, i):
    Bn, L, _ = h.shape
    z = (h @ p['gdn_w_in'][i]).astype(jnp.float32)
    qkv, b_in, a_in, zg = jnp.split(z, (N_QKV_C, N_QKV_C + H_C, N_QKV_C + 2 * H_C), axis=-1)
    xp = jnp.concatenate([conv_prev.astype(jnp.float32), qkv], axis=1)
    cw = p['gdn_conv_w'][i]
    conv = xp[:, 0:L] * cw[0]
    for j in range(1, CONV_W):
        conv = conv + xp[:, j:j + L] * cw[j]
    qkv = jax.nn.silu(conv)
    q, k, v = jnp.split(qkv, (H_C * DK_C, 2 * H_C * DK_C), axis=-1)
    q = l2_normalize(q.reshape(Bn, L, H_C, DK_C))
    k = l2_normalize(k.reshape(Bn, L, H_C, DK_C))
    v = v.reshape(Bn, L, H_C, DV_C)
    beta = jax.nn.sigmoid(b_in)
    g = -jnp.exp(p['gdn_A_log'][i]) * jax.nn.softplus(a_in + p['gdn_dt_bias'][i])
    o, S = gated_delta_chunked(q, k, v, g, beta, S0)
    o = (o * lax.rsqrt(jnp.mean(o * o, -1, keepdims=True) + 1e-6) * p['gdn_norm_g'][i]
         * jax.nn.silu(zg.reshape(Bn, L, H_C, DV_C)))
    return o.reshape(Bn, L, C_C) @ p['gdn_w_out'][i], xp[:, L:], S

def trunk(x, pos0, states, p):
    st_shift, st_rwkv, st_ret, st_conv, st_gdn = states
    pos = pos0 + jnp.arange(x.shape[1], dtype=jnp.float32)
    new_shift, new_rwkv, new_ret, new_conv, new_gdn = [], [], [], [], []
    h = x
    for l in range(DEPTH):
        i = l // 2
        f = swiglu(h, p['ffn_w_gate'][l, 0], p['ffn_w_up'][l, 0], p['ffn_w_down'][l, 0])
        h = layer_norm(DEEPNORM_ALPHA * h + 0.5 * f, p['ln_g'][l, 0], p['ln_b'][l, 0])
        if l % 2 == 0:
            m, s_sh, s_rw, s_rt = ab_mixer(h, pos, st_shift[i], st_rwkv[i], st_ret[i], p, i)
            new_shift.append(s_sh)
            new_rwkv.append(s_rw)
            new_ret.append(s_rt)
        else:
            m, s_cv, s_gd = gdn_mixer(h, st_conv[i], st_gdn[i], p, i)
            new_conv.append(s_cv)
            new_gdn.append(s_gd)
        h = layer_norm(DEEPNORM_ALPHA * h + m, p['ln_g'][l, 1], p['ln_b'][l, 1])
        f = swiglu(h, p['ffn_w_gate'][l, 1], p['ffn_w_up'][l, 1], p['ffn_w_down'][l, 1])
        h = layer_norm(DEEPNORM_ALPHA * h + 0.5 * f, p['ln_g'][l, 2], p['ln_b'][l, 2])
    return h, (jnp.stack(new_shift), jnp.stack(new_rwkv), jnp.stack(new_ret),
               jnp.stack(new_conv), jnp.stack(new_gdn))

def setup_inputs(seed: int = 0) -> dict:
    key = jax.random.key(seed)
    ks = iter(jax.random.split(key, 40))
    f32 = jnp.float32
    nrm = lambda shape, scale: jax.random.normal(next(ks), shape, f32) * scale
    uni = lambda shape, lo, hi: jax.random.uniform(next(ks), shape, f32, lo, hi)
    d = {}
    d['x_prompt'] = nrm((BATCH, SEQ, D_MODEL), 1.0)
    d['x_sample'] = nrm((DEC_BATCH, DEC_SEQ, D_MODEL), 1.0)
    d['state_rwkv_shift'] = nrm((N_AB_LAYERS, DEC_BATCH, A_SHIFT_COLS), 1.0)
    d['state_rwkv'] = nrm((N_AB_LAYERS, DEC_BATCH, H_A, N_A, N_A), 0.3)
    d['state_ret'] = nrm((N_AB_LAYERS, DEC_BATCH, H_B, DK_B, DV_B), 0.3)
    d['state_gdn_conv'] = nrm((N_C_LAYERS, DEC_BATCH, CONV_W - 1, N_QKV_C), 1.0)
    d['state_gdn'] = nrm((N_C_LAYERS, DEC_BATCH, H_C, DK_C, DV_C), 0.3)
    d['ln_g'] = 1.0 + nrm((DEPTH, 3, D_MODEL), 0.02)
    d['ln_b'] = nrm((DEPTH, 3, D_MODEL), 0.02)
    d['ffn_w_gate'] = nrm((DEPTH, 2, D_MODEL, D_FF), D_MODEL ** -0.5)
    d['ffn_w_up'] = nrm((DEPTH, 2, D_MODEL, D_FF), D_MODEL ** -0.5)
    d['ffn_w_down'] = nrm((DEPTH, 2, D_FF, D_MODEL), D_FF ** -0.5 * DEEPNORM_BETA)
    d['ab_w_in'] = nrm((N_AB_LAYERS, D_MODEL, AB_COLS), D_MODEL ** -0.5)
    d['ab_w_out'] = nrm((N_AB_LAYERS, C_A + C_B, D_MODEL), (C_A + C_B) ** -0.5 * DEEPNORM_BETA)
    d['rwkv_mu'] = uni((N_AB_LAYERS, A_SHIFT_COLS), 0.0, 1.0)
    d['rwkv_w0'] = jnp.linspace(-5.0, 1.0, C_A, dtype=f32)[None, :] + nrm((N_AB_LAYERS, C_A), 0.1)
    d['rwkv_w2'] = nrm((N_AB_LAYERS, W_LORA, C_A), W_LORA ** -0.5 * 0.3)
    d['rwkv_a0'] = nrm((N_AB_LAYERS, C_A), 0.3)
    d['rwkv_a2'] = nrm((N_AB_LAYERS, A_LORA, C_A), A_LORA ** -0.5 * 0.3)
    d['rwkv_g2'] = nrm((N_AB_LAYERS, G_LORA, C_A), G_LORA ** -0.5)
    d['rwkv_k_k'] = 0.85 + nrm((N_AB_LAYERS, C_A), 0.05)
    d['rwkv_k_a'] = 1.0 + nrm((N_AB_LAYERS, C_A), 0.05)
    d['rwkv_r_k'] = nrm((N_AB_LAYERS, H_A, N_A), 0.1)
    d['rwkv_gn_g'] = 1.0 + nrm((N_AB_LAYERS, C_A), 0.02)
    d['rwkv_gn_b'] = nrm((N_AB_LAYERS, C_A), 0.02)
    d['ret_gn_g'] = 1.0 + nrm((N_AB_LAYERS, C_B), 0.02)
    d['ret_gn_b'] = nrm((N_AB_LAYERS, C_B), 0.02)
    d['gdn_w_in'] = nrm((N_C_LAYERS, D_MODEL, C_COLS), D_MODEL ** -0.5)
    d['gdn_conv_w'] = nrm((N_C_LAYERS, CONV_W, N_QKV_C), 0.5)
    d['gdn_A_log'] = jnp.log(uni((N_C_LAYERS, H_C), 1.0, 16.0))
    dt = jnp.exp(uni((N_C_LAYERS, H_C), float(np.log(1e-3)), float(np.log(1e-1))))
    d['gdn_dt_bias'] = dt + jnp.log(-jnp.expm1(-dt))
    d['gdn_norm_g'] = 1.0 + nrm((N_C_LAYERS, DV_C), 0.02)
    d['gdn_w_out'] = nrm((N_C_LAYERS, C_C, D_MODEL), C_C ** -0.5 * DEEPNORM_BETA)
    return d

def reference(x_prompt, x_sample, state_rwkv_shift, state_rwkv, state_ret, state_gdn_conv, state_gdn,
              ln_g, ln_b, ffn_w_gate, ffn_w_up, ffn_w_down, ab_w_in, ab_w_out, rwkv_mu, rwkv_w0,
              rwkv_w2, rwkv_a0, rwkv_a2, rwkv_g2, rwkv_k_k, rwkv_k_a, rwkv_r_k, rwkv_gn_g, rwkv_gn_b,
              ret_gn_g, ret_gn_b, gdn_w_in, gdn_conv_w, gdn_A_log, gdn_dt_bias, gdn_norm_g, gdn_w_out):
    p = dict(ln_g=ln_g, ln_b=ln_b, ffn_w_gate=ffn_w_gate, ffn_w_up=ffn_w_up, ffn_w_down=ffn_w_down,
             ab_w_in=ab_w_in, ab_w_out=ab_w_out, rwkv_mu=rwkv_mu, rwkv_w0=rwkv_w0, rwkv_w2=rwkv_w2,
             rwkv_a0=rwkv_a0, rwkv_a2=rwkv_a2, rwkv_g2=rwkv_g2, rwkv_k_k=rwkv_k_k, rwkv_k_a=rwkv_k_a,
             rwkv_r_k=rwkv_r_k, rwkv_gn_g=rwkv_gn_g, rwkv_gn_b=rwkv_gn_b, ret_gn_g=ret_gn_g,
             ret_gn_b=ret_gn_b, gdn_w_in=gdn_w_in, gdn_conv_w=gdn_conv_w, gdn_A_log=gdn_A_log,
             gdn_dt_bias=gdn_dt_bias, gdn_norm_g=gdn_norm_g, gdn_w_out=gdn_w_out)
    nb = x_prompt.shape[0]
    zeros = lambda shape: jnp.zeros(shape, jnp.float32)
    empty = (zeros((N_AB_LAYERS, nb, A_SHIFT_COLS)), zeros((N_AB_LAYERS, nb, H_A, N_A, N_A)),
             zeros((N_AB_LAYERS, nb, H_B, DK_B, DV_B)), zeros((N_C_LAYERS, nb, CONV_W - 1, N_QKV_C)),
             zeros((N_C_LAYERS, nb, H_C, DK_C, DV_C)))
    y_prompt, (p_shift, p_rwkv, p_ret, p_conv, p_gdn) = trunk(x_prompt, 0, empty, p)
    past = (state_rwkv_shift, state_rwkv, state_ret, state_gdn_conv, state_gdn)
    y_sample, (s_shift, s_rwkv, s_ret, s_conv, s_gdn) = trunk(x_sample, PAST_LEN, past, p)
    return (y_prompt, y_sample, p_shift, p_rwkv, p_ret, p_conv, p_gdn, s_shift, s_rwkv, s_ret, s_conv, s_gdn)


_drawn_inputs = setup_inputs


def setup_inputs(seed=0):
    import zlib

    import numpy as np

    out = dict(_drawn_inputs(seed))
    spreads = {}
    factors = {'rwkv_w2': 3.318,
     'rwkv_gn_g': 26.388,
     'rwkv_gn_b': 21.593,
     'ret_gn_g': 22.421,
     'ret_gn_b': 23.315,
     'gdn_norm_g': 75.516,
     'rwkv_r_k': 5.6}
    for name, (base, spread) in spreads.items():
        noise = np.random.default_rng([zlib.crc32(name.encode()), seed]).standard_normal(out[name].shape)
        drawn = base * np.exp(spread * noise) if base else spread * noise
        out[name] = __import__('jax').numpy.asarray(drawn.astype(out[name].dtype))
    for name, factor in factors.items():
        out[name] = (out[name] * factor).astype(out[name].dtype)
    return out
```

```python
from contextlib import ExitStack

import numpy as np
import concourse.bass as bass
from concourse import mybir

F32 = mybir.dt.float32
F32R = mybir.dt.float32r
ALU = mybir.AluOpType
ACT = mybir.ActivationFunctionType

P = 128
D = 1024
DT = D // P
SEQ, DB, DS = 256, 8, 4
NS = DB * DS
T = SEQ + NS
F = 2816
FT = F // P
ALPHA = 4.0 ** 0.25
LN_EPS = 1e-5
RWKV_EPS = 64e-5
RET_EPS = 1e-5
CH = 64
LEVELS = 6
HA, HB, HC = 8, 4, 8
ZA, ZB = 14, 16
QKV = 24
PADW = 3 + SEQ + DB * 7
CONVW = PADW - 3
EM05 = float(np.exp(-0.5))
QSCALE = float(128.0 ** -0.5)

UW1 = 8 * P
UW2 = 11 * P
RAW, SPL = 4, 2
STAGES = []
for _f, _m in ((0, None), (None, "ab"), (1, None), (2, None), (None, "gdn"), (3, None)):
    if _f is not None:
        STAGES += [(f"up{_f}", "up", 2 * FT), (f"down{_f}", "down", 2 * DT)]
    elif _m == "ab":
        STAGES += [("za", "za", ZA), ("zb", "zb", ZB), ("abo", "abo", DT)]
    else:
        STAGES += [("ba", "ba", 1), ("qk", "conv", 16), ("v", "conv", 8), ("zg", "gate", 8), ("gdo", "out", DT)]


SPLIT_FIRST = ("conv", "gate", "za", "zb")
WRITTEN_OUT = ("za", "zb", "abo")
WARM = 16
ZA_ORDER = [12, 13, 4, 5, 6, 7, 0, 1, 2, 3, 8, 9, 10, 11]
ZPW = 1 + SEQ + DB * 5


def layout_constants():
    s = np.arange(P)[:, None]
    t = np.arange(P)[None, :]
    f = np.float32
    allc, ab, gd = {}, {}, {}
    allc["ident"] = np.eye(P)
    allc["ones"] = np.ones((P, P))
    allc["mean"] = np.full((P, P), 1.0 / D)
    for nm, ch, w in (("up64", CH, P), ("up4", DS, NS)):
        same = s // ch == t // ch
        allc[nm] = np.concatenate([(same & (s < t))[:, :w], (same & (s <= t))[:, :w]], 1)
    for l in range(LEVELS):
        b = 2 ** l
        allc[f"lev{l}"] = (s // (2 * b) == t // (2 * b)) & (s % (2 * b) < b) & (t % (2 * b) >= b)
    allc["low0"] = allc["lev0"].T
    first = np.zeros(T, bool)
    first[0:SEQ:CH] = True
    first[SEQ::DS] = True
    allc["scan"] = np.tile(np.where(first, 0.0, 1.0)[None], (P, 1))
    allc["selb"] = (s // DS == np.arange(DB)[None, :])
    allc["eps"] = np.tile(np.array([LN_EPS, 4 * LN_EPS, RWKV_EPS, RET_EPS, 1e-6, 1.0])[None], (P, 1))

    ab["blk"] = (s // 64 == t // 64)
    ab["id64"] = (s % 64 == np.arange(64)[None, :])
    ab["rot"] = np.zeros((P, P))
    for i in range(64):
        ab["rot"][i + 64, i] = -1.0
        ab["rot"][i, i + 64] = 1.0
    half = np.linspace(0.0, 1.0, 64, dtype=f)
    inv = (f(1.0) / (f(10000.0) ** half)).astype(f)
    pos = np.concatenate([np.arange(SEQ), np.tile(2048 + np.arange(DS), DB)]).astype(f)
    ang = (pos[None, :] * inv[:, None]).astype(f)
    ab["cos"] = np.tile(np.cos(ang.astype(np.float64)), (2, 1))
    ab["sin"] = np.tile(np.sin(ang.astype(np.float64)), (2, 1))
    lg = np.log(1.0 - 2.0 ** (-5.0 - np.arange(HB)))
    ab["rdec"] = np.concatenate([np.where(s <= t, np.exp((t - s) * lg[h]), 0.0) for h in range(HB)], 1)
    t4 = t[:, :NS]
    ab["rdec4"] = np.concatenate([np.where((s // 4 == t4 // 4) & (s <= t4), np.exp((t4 - s) * lg[h]), 0.0)
                                  for h in range(HB)], 1)
    ab["zeta"] = np.concatenate([np.exp((127.0 - s) * lg[h]) for h in range(HB)], 1)
    ab["zeta4"] = np.concatenate([np.exp((3.0 - s % 4) * lg[h]) for h in range(HB)], 1)
    ab["xi"] = np.concatenate([np.tile(np.exp((np.arange(P) + 1.0) * lg[h])[None], (P, 1)) for h in range(HB)], 1)
    ab["xi4"] = np.concatenate([np.tile(np.exp((np.arange(NS) % 4 + 1.0) * lg[h])[None], (P, 1))
                                for h in range(HB)], 1)

    gd["sel8"] = (s[:, :, None] % 32 == np.arange(HC)[None, :, None]) * np.ones((1, 1, P))
    where, arrays = {}, []
    for group in (allc, ab, gd):
        at, parts = 0, []
        for k, v in group.items():
            a = np.asarray(v, np.float64).reshape(P, -1).astype(f)
            where[k] = (at, a.shape[1])
            at += a.shape[1]
            parts.append(a)
        arrays.append(np.ascontiguousarray(np.concatenate(parts, 1)))
    return where, arrays


CAT, (CONST_ALL, CONST_AB, CONST_GD) = layout_constants()
GAMMA = [float(1.0 - 2.0 ** (-5.0 - h)) for h in range(HB)]

PCOLS = {}
_at = 0
for _n, _w in (("ln_g", 48), ("ln_b", 48), ("mu", ZA), ("w0", 4), ("a0", 4), ("kk", 4), ("ka", 4), ("rk", 4),
               ("gng", 4), ("gnb", 4), ("rgg", 4), ("rgb", 4), ("conv", 4 * QKV), ("ng", 1), ("alog", 1),
               ("dtb", 1)):
    PCOLS[_n] = (_at, _w)
    _at += _w
NPAR = _at

JOB_BANKS = 4


NAT_ORDER = (0, 3, 1, 2)


def plan_jobs():
    jobs = []

    def norm(n):
        jobs.extend([("mean", n), ("var", n)])

    def invert(tag, j):
        for l in range(1, LEVELS):
            jobs.extend(("Y", tag, j, s, l) for s in range(2))
            for s in range(2):
                if l < LEVELS - 1:
                    jobs.append(("X", tag, j, s, l))
                jobs.append(("XT", tag, j, s, l))

    norm(0)
    jobs.extend((k, t) for k in ("lora_w", "lora_a", "gate") for t in range(4))
    jobs.extend(("l2", t) for t in range(4))
    jobs.extend(("bonus", t) for t in range(4))
    jobs.extend(("nat", j, m) for m in NAT_ORDER for j in range(3))
    for j in range(2):
        for s in range(2):
            jobs.extend(("gram", j, s, h) for h in range(4))
            jobs.extend(("gramL", j, s, e) for e in range(2))
        jobs.extend(("MV", j, s) for s in range(2))
        invert("a", j)
        for s in range(2):
            jobs.extend([("UW", j, s), ("O0", j, s), ("Q1", j, s)])
            jobs.extend((k, j, s, c) for k in ("G", "H") for c in range(2))
    jobs.extend(("chain", c, e) for c in range(1, 4) for e in range(2))
    jobs.extend(("OS", q, e) for q in range(2) for e in range(2))
    jobs.extend([("sgram", 0), ("sgram", 1), ("sgramL", 0), ("sgramL", 1), ("sY", 0), ("sXT", 0), ("sMV", 0),
                 ("sX", 0), ("sX", 1), ("sU", 0), ("sO", 0), ("sOS", 0), ("sOS", 1)])
    jobs.extend(("sS", t) for t in range(4))
    jobs.extend((k, t) for k in ("gnm", "gnv") for t in range(4))
    jobs.extend(("rot", t) for t in range(8))
    jobs.extend([("rkn", 0), ("rkn", 1), ("rkn", 2), ("rQ", 0), ("rvn", 0), ("rvn", 1), ("rQ", 1), ("rvn", 2),
                 ("ratt", 0), ("rQ", 2), ("ratt", 1), ("rQ", 3), ("rsatt", 0), ("rS", 0), ("rS", 1)])
    jobs.extend([("rO", 0), ("rO", 1), ("rgm", 0), ("rO", 2), ("rgm", 1), ("rgv", 0), ("rO", 3), ("rgm", 2),
                 ("rgv", 1), ("rgm", 3), ("rgv", 2), ("rgv", 3)])
    jobs.extend(("rsS", h, q) for h in range(4) for q in range(2))
    norm(1)
    norm(2)
    norm(3)
    jobs.extend([("gtokb", 0), ("gtok", 0)])
    jobs.extend(("dl2", t) for t in range(16))
    for s in range(2):
        if s == 0:
            jobs.extend((k, s, h) for k in ("dgb", "dbb") for h in range(4))
        for j in range(2):
            jobs.extend([("dgram", s, j, q) for q in range(3)])
        for l in range(1, LEVELS):
            jobs.extend(("dY", s, j, l) for j in range(2))
            if l < 4:
                jobs.extend([("dvn", s, l - 1), ("dkn", s, l - 1)])
            for j in range(2):
                if l < LEVELS - 1:
                    jobs.append(("dX", s, j, l))
                jobs.append(("dXT", s, j, l))
        for j in range(2):
            jobs.extend([("dUW", s, j, 0), ("dUW", s, j, 1), ("dO0", s, j), ("dQ1", s, j),
                         ("dG", s, j, 0), ("dG", s, j, 1), ("dH", s, j, 0), ("dH", s, j, 1)])
        jobs.extend(("dchain", s, c) for c in range(1, 4))
        jobs.extend(("dOS", s, q) for q in range(4))
        if s == 0:
            jobs.extend(("dgb", 1, h) for h in range(4))
        jobs.append(("dsX", s))
        jobs.extend([("dsgram", s, q) for q in range(3)])
        jobs.extend([("dsY", s), ("dsXT", s), ("dsU", s), ("dsO", s), ("dsT", s)])
        if s == 0:
            jobs.extend(("dbb", 1, h) for h in range(4))
            jobs.extend(("dnrm", t) for t in range(4))
        jobs.extend(("dsS", s, 0, q) for q in range(2))
        if s == 1:
            jobs.extend(("dnrm", t) for t in range(4, 8))
        jobs.extend(("dsS", s, h, q) for h in range(1, 4) for q in range(2))
    norm(4)
    norm(5)
    return {k: n for n, k in enumerate(jobs)}


JOBS = plan_jobs()


def bank_of(key):
    return JOBS[key] % JOB_BANKS


def uses_before(key):
    return JOBS[key] // JOB_BANKS


def stage_table():
    table, unit, uses = {}, 0, [0, 0, 0, 0]
    for name, kind, n in STAGES:
        table[name] = (kind, n, unit, list(uses))
        for k in range(n):
            if kind != "down" or k % 2 == 0:
                uses[k % 4] += 1
        unit += n
    return table, unit, uses


TABLE, UNITS, _ = stage_table()
FIRST_UNIT = {}
for _name, (_kind, _n, _u, _) in TABLE.items():
    for _k in range(_n):
        FIRST_UNIT[_u + _k] = (_name, _kind, _k)

W1_ROW, W2_ROW = {}, {}
_a = _b = 0
for _name, _kind, _n in STAGES:
    if _kind == "down":
        W2_ROW[_name] = _b
        _b += _n
    else:
        W1_ROW[_name] = _a
        _a += _n
N_W1, N_W2 = _a, _b

PHASES = ["ffn0", "norm0", "ab0", "norm1", "ffn1", "norm2", "ffn2", "norm3", "gdn0", "norm4", "ffn3", "norm5"]
PHASE_STAGES = {ph: ([f"up{ph[3]}", f"down{ph[3]}"] if ph[:3] == "ffn" else []) for ph in PHASES}
PHASE_STAGES["ab0"] = ["za", "zb", "abo"]
PHASE_STAGES["gdn0"] = ["ba", "qk", "v", "zg", "gdo"]
NORM_STAGE = {0: "down0", 1: "abo", 2: "down1", 3: "down2", 4: "gdo", 5: "down3"}
X_VERSION = {0: 1, 1: 3, 2: 4, 3: 5, 4: 7}
FFN_VERSION = {0: 0, 1: 3, 2: 4, 3: 7}
MIX_NAMES = {"blk", "id64", "rot", "cos", "sin", "rdec", "rdec4", "zeta", "zeta4", "xi", "xi4", "sel8"}

M_COLS = 25728
A_Z, A_KT, A_BATCH = 0, 0, 1152
A_A, A_CUM, A_EIN, A_EE = 4736, 5888, 7040, 8192
A_LD, A_KK, A_TB, A_GATE = 9344, 10496, 11648, 12800
A_NAT, A_XK, A_GT, A_H, A_S, A_PC, A_LC, A_SH = 13952, 18560, 21632, 22656, 23680, 24704, 24752, 24880
A_KB, A_S0, A_SAT, A_SX = A_NAT, A_XK, A_GT, A_KK
B_Z, B_S0, B_VN, B_KZ, B_AT, B_SAT, B_S, B_OT, B_QX, B_VB = \
    0, 4608, 13952, 15488, 17024, 18048, 18176, 19200, 20352, 21504
G_C, G_ZG, G_RAW, G_ACC, G_CIN = 0, 6912, 9216, 16776, 17400
G_L2, G_SQ = 19200, 22528
G_XK, G_KD, G_GT, G_H, G_S, G_BATCH = 9216, 12288, 13824, 15872, 17920, 19456
G_COUT = 18000


def delta_kernel(nc, a):
    ctx = ExitStack()
    with ctx:
        def sb(name, cols, dt=F32):
            return ctx.enter_context(nc.sbuf_tensor(name, [P] + list(cols), dt))

        _sems = {}

        def sem(name):
            if name not in _sems:
                _sems[name] = ctx.enter_context(nc.semaphore(name))
            return _sems[name]

        raw = [sb(f"raw{i}", [UW2]) for i in range(RAW)]
        whi = [sb(f"whi{i}", [UW2], F32R) for i in range(SPL)]
        wlo = [sb(f"wlo{i}", [UW2], F32R) for i in range(SPL)]
        x = sb("x", [DT, T])
        with ExitStack() as region:
            xhi = region.enter_context(nc.sbuf_tensor("xhi", [P, DT, T], F32R))
            xlo = region.enter_context(nc.sbuf_tensor("xlo", [P, DT, T], F32R))
        s0_space = sb("s0_space", [2 * DT * T])
        xsum = sb("xsum", [T])
        act_scratch = sb("act_scratch", [2])
        r = sb("r", [DT * T])
        cst = sb("cst", [CONST_ALL.shape[1]])
        mixc = sb("mixc", [3240])
        par = sb("par", [NPAR])
        with ExitStack() as region:
            hhi = region.enter_context(nc.sbuf_tensor("hhi", [P, FT, T], F32R))
            hlo = region.enter_context(nc.sbuf_tensor("hlo", [P, FT, T], F32R))
            sg = region.enter_context(nc.sbuf_tensor("sg", [P, 2, T], F32))
            hb = region.enter_context(nc.sbuf_tensor("hb", [P, 2, T], F32))
        M = ctx.enter_context(nc.sbuf_tensor("M", [P, M_COLS], F32))
        r3 = r[:].rearrange("p (d t) -> p d t", d=DT)
        kr = r[:].rearrange("p (t x s) -> p t x s", t=4, x=2)

        gemm = [ctx.enter_context(nc.psum_tensor(f"gemm{i}", [P, 512], F32)) for i in range(4)]
        jobb = [ctx.enter_context(nc.psum_tensor(f"job{i}", [P, 512], F32)) for i in range(JOB_BANKS)]

        raw_in = [sem(f"raw_in{i}") for i in range(RAW)]
        hi_ready, lo_ready = sem("hi_ready"), sem("lo_ready")
        unit_done = sem("unit_done")
        bank_free = [sem(f"bank_free{i}") for i in range(4)]
        filled = [sem(f"filled{i}") for i in range(JOB_BANKS)]
        drained = [sem(f"drained{i}") for i in range(JOB_BANKS)]
        x_hi, x_lo = sem("x_hi"), [sem("x_lo_even"), sem("x_lo_odd")]
        hid_hi, hid_lo = sem("hid_hi"), sem("hid_lo")

        def C(name, rows=slice(0, P)):
            at, w = CAT[name]
            src = mixc if name in MIX_NAMES else cst
            return src[rows, at:at + w]

        def pc(name, i=0, rows=slice(0, P)):
            at, _ = PCOLS[name]
            return par[rows, at + i:at + i + 1]

        def m(at, *dims, rows=slice(0, P)):
            n = int(np.prod(dims))
            ap = M[rows, at:at + n]
            names = "abcd"[:len(dims)]
            if len(dims) == 1:
                return ap
            return ap.rearrange("p (" + " ".join(names) + ") -> p " + " ".join(names),
                                **dict(zip(names, dims)))

        def full(key):
            return filled[bank_of(key)], uses_before(key) + 1

        def empty(key):
            return drained[bank_of(key)], uses_before(key)

        def out(key):
            return drained[bank_of(key)], uses_before(key) + 1

        def stage_read(eng, stage):
            kind, n, u0, use = TABLE[stage]
            for b in range(4):
                mine = sum(1 for k in range(n) if k % 4 == b and (kind != "down" or k % 2 == 0))
                if mine:
                    eng.wait_ge(bank_free[b], use[b] + mine)

        def wait_count(eng, s, count):
            if not isinstance(count, int) or count > 0:
                eng.wait_ge(s, count)

        def low_parts(eng, ops, version, first, src):
            for d in range(first, DT, 2):
                eng.wait_ge(x_hi, DT * version + d + 1)
                ops.tensor_tensor(xlo[:, d, :], src(d), xhi[:, d, :].bitcast(F32), ALU.subtract
                                  ).then_inc(x_lo[first], 1)

        def bc(ap, dim, n):
            v = ap.unsqueeze(dim)
            shape = list(v.shape)
            shape[dim] = n
            return v.to_broadcast(shape)

        def units(eng, n, body, peel=False, loop=True):
            loops = max((n - 2) // 4, 0) if loop else 0
            first = 1 if peel and loops else 0
            for j in range(4 * first):
                body(0, j)
            if loops > first:
                with eng.Fori(first, loops) as i:
                    for j in range(4):
                        body(i, j)
            for k in range(4 * loops, n):
                body(k // 4, k % 4)

        AT = [m(A_BATCH + 4096 * s, 4, 512) for s in range(2)]
        TM = [m(A_BATCH + 4096 * s + 2048, 4, P) for s in range(2)]
        TT = [m(A_BATCH + 4096 * s + 2560, 4, P) for s in range(2)]
        YM = [m(A_BATCH + 4096 * s + 3072, 4, P) for s in range(2)]
        AM = [m(A_BATCH + 4096 * s + 3584, 4, P) for s in range(2)]
        a_z = m(A_Z, ZA, T)
        a_kt, a_a, a_cum, a_ein, a_ee = (m(o, 4, T) for o in (A_KT, A_A, A_CUM, A_EIN, A_EE))
        a_ld, a_kk, a_tb, a_gate = (m(o, 4, T) for o in (A_LD, A_KK, A_TB, A_GATE))
        a_nat = m(A_NAT, 3, 3, 512)
        a_xk = m(A_XK, 3, 8, P)
        a_zp = m(A_NAT, ZA, ZPW)
        a_dz = m(A_XK, 2, ZPW)
        a_km = m(A_XK + 600, 4)
        a_k1, a_rk = m(A_XK + 640, 4, T), m(A_XK + 1792, 4, T)
        a_gt, a_h = m(A_GT, 4, 4, 64), m(A_H, 4, 4, 64)
        a_s = m(A_S, 4, 4, 64)
        a_pc = m(A_PC, 4, 12)
        a_lc, a_sh = m(A_LC, ZA, 9), m(A_SH, ZA, DB)
        a_s0 = m(A_S0, 4, DB, 64)
        a_kb = m(A_KB, 4, 544)
        s_at = m(A_SAT, 8, P, rows=slice(0, NS))
        s_t, s_tt, s_y, s_a = (m(A_SAT + 1024 + 256 * i, 8, NS, rows=slice(0, NS)) for i in range(4))
        s_x, s_u = (m(A_SX + 512 * i, 8, 64, rows=slice(0, NS)) for i in range(2))
        s_vb, s_ub = (m(A_BATCH + 4096 * i, 8, DB, 64, rows=slice(0, NS)) for i in range(2))
        g2w2 = mixc[:, CONST_AB.shape[1]:CONST_AB.shape[1] + 1024]
        NROW = slice(0, NS)

        def halves(h):
            return h // 2, slice(64 * (h % 2), 64 * (h % 2) + 64)

        def tok(j):
            return slice(P * j, P * j + (P if j < 2 else NS))

        def mask4(name, w, rows=slice(0, P)):
            return bc(C(name, rows)[:, 0:w], 1, 4)

        def masked_count(j, s, l):
            return (j * (LEVELS - 1) + l - 1) * 2 + s + 1

        b_z = m(B_Z, ZB, T)
        b_s0 = m(B_S0, 4, DB, P)
        b_vn, b_kz = m(B_VN, 3, 4, P), m(B_KZ, 3, 4, P)
        b_at = m(B_AT, 2, 4, P)
        b_sat = m(B_SAT, 4, NS, rows=NROW)
        b_s = m(B_S, 2, 4, P)
        b_ot, b_qx = m(B_OT, 4, T), m(B_QX, 4, T)
        b_vb = m(B_VB, 4, DB, P, rows=NROW)
        a_rs = m(A_GT, 4, T)
        b_rt = r[:].rearrange("p (d t) -> p d t", d=8)

        def ab_tensor(pe, env):
            start, stage = env["start"], env["stage"]

            def fin(ins, key):
                ins.then_inc(filled[bank_of(key)], 1)

            def lora(name, rows, tile, w0):
                for t in range(4):
                    bank = start((name, t))
                    fin(pe.matmul(bank[:, 0:T], g2w2[rows, w0 + t * P:w0 + (t + 1) * P], a_z[rows, tile, :],
                                  start=True, stop=True), (name, t))

            def behind(k):
                if k == 4:
                    pe.wait_ge(sem("const_in"), 64)
                    pe.wait_ge(sem("lora_act"), 1)
                    lora("lora_w", slice(0, 64), 12, 0)
                elif k == 5:
                    lora("lora_a", slice(64, P), 12, 0)
                elif k == 6:
                    pe.wait_ge(sem("lora_act"), 2)
                    lora("gate", slice(0, P), 13, 512)
                elif k == 7:
                    pe.wait_ge(sem("ksq"), 1)
                    for t in range(4):
                        bank = start(("l2", t))
                        fin(pe.matmul(bank[:, 0:T], C("blk"), a_tb[:, t, :], start=True, stop=True), ("l2", t))

            stage("za", 1, behind)
            pe.wait_ge(sem("rk"), 1)
            for t in range(4):
                bank = start(("bonus", t))
                fin(pe.matmul(bank[:, 0:T], C("blk"), a_rk[:, t, :], start=True, stop=True), ("bonus", t))
            for mt in NAT_ORDER:
                if mt == 0:
                    pe.wait_ge(sem("shifted"), 14)
                elif mt == 3:
                    pe.wait_ge(sem("kk_prev"), 1)
                elif mt == 1:
                    pe.wait_ge(sem("operands"), 1)
                else:
                    pe.wait_ge(sem("operands_pool"), 1)
                for j in range(3):
                    w = P if j < 2 else NS
                    bank = start(("nat", j, mt))
                    for t in range(4):
                        src = (a_z[:, 8 + t, tok(j)], a_z[:, 4 + t, tok(j)], a_a[:, t, tok(j)],
                               kr[:, t, 0, tok(j)])[mt]
                        mm = pe.transpose(bank[0:w, t * P:(t + 1) * P], src, C("ident"))
                    fin(mm, ("nat", j, mt))
            for j in range(2):
                for s in range(2):
                    for h in range(4):
                        t, po = halves(4 * s + h)
                        bank = start(("gram", j, s, h))
                        pe.matmul(bank[:, 0:256], a_kk[po, t, tok(j)], kr[po, t, :, tok(j)], start=True, stop=True)
                        fin(pe.matmul(bank[:, 256:512], a_kt[po, t, tok(j)], kr[po, t, :, tok(j)],
                                      start=True, stop=True), ("gram", j, s, h))
                    for e in range(2):
                        bank = start(("gramL", j, s, e))
                        for q in range(2):
                            t, po = halves(4 * s + 2 * q + e)
                            mm = pe.matmul(bank[:, q * P:(q + 1) * P], kr[po, t, 0, tok(j)], a_kk[po, t, tok(j)],
                                           start=True, stop=True)
                        fin(mm, ("gramL", j, s, e))
                for s in range(2):
                    bank = start(("MV", j, s))
                    pe.wait_ge(*out(("nat", j, 0)))
                    pe.wait_ge(*out(("gram", j, s, 3)))
                    for h in range(4):
                        hd = 4 * s + h
                        mm = pe.matmul(bank[:, h * 64:(h + 1) * 64], AT[s][:, h, 256:384],
                                       a_nat[:, j, 0, hd * 64:(hd + 1) * 64], start=True, stop=True)
                    fin(mm, ("MV", j, s))
                invert_tensor(pe, start, fin, "a", j, TM, TT, YM, AM)
                for s in range(2):
                    bank = start(("UW", j, s))
                    pe.wait_ge(*out(("XT", "a", j, s, LEVELS - 1)))
                    pe.wait_ge(*out(("MV", j, s)))
                    pe.wait_ge(*out(("nat", j, 3)))
                    for h in range(4):
                        mm = pe.matmul(bank[:, h * P:(h + 1) * P], TT[s][:, h, :], a_xk[:, j, 4 * s + h, :],
                                       start=True, stop=True)
                    fin(mm, ("UW", j, s))
                    bank = start(("O0", j, s))
                    pe.wait_ge(*out(("UW", j, s)))
                    pe.wait_ge(*out(("nat", j, 1)))
                    pe.wait_ge(*out(("nat", j, 2)))
                    for h in range(4):
                        hd = 4 * s + h
                        po, q = halves(hd)[1], h // 2
                        pe.matmul(bank[po, q * P:(q + 1) * P], a_nat[:, j, 0, hd * 64:(hd + 1) * 64],
                                  AT[s][:, h, 384:512], start=True, stop=False)
                        mm = pe.matmul(bank[po, q * P:(q + 1) * P], a_xk[:, j, hd, 0:64], AT[s][:, h, 128:256],
                                       start=False, stop=True)
                    fin(mm, ("O0", j, s))
                    bank = start(("Q1", j, s))
                    for h in range(4):
                        hd = 4 * s + h
                        po, q = halves(hd)[1], h // 2
                        mm = pe.matmul(bank[po, q * P:(q + 1) * P], a_xk[:, j, hd, 64:128], AT[s][:, h, 128:256],
                                       start=True, stop=True)
                    fin(mm, ("Q1", j, s))
                    for c in range(2):
                        bank = start(("G", j, s, c))
                        for h in range(4):
                            hd = 4 * s + h
                            po, q = halves(hd)[1], h // 2
                            rows = slice(64 * c, 64 * c + 64)
                            mm = pe.matmul(bank[po, q * 64:q * 64 + 64], a_xk[rows, j, hd, 64:128],
                                           a_nat[rows, j, 2, hd * 64:(hd + 1) * 64], start=True, stop=True)
                        fin(mm, ("G", j, s, c))
                    for c in range(2):
                        bank = start(("H", j, s, c))
                        for h in range(4):
                            hd = 4 * s + h
                            po, q = halves(hd)[1], h // 2
                            rows = slice(64 * c, 64 * c + 64)
                            pe.matmul(bank[po, q * 64:q * 64 + 64], a_nat[rows, j, 1, hd * 64:(hd + 1) * 64],
                                      a_nat[rows, j, 0, hd * 64:(hd + 1) * 64], start=True, stop=False)
                            mm = pe.matmul(bank[po, q * 64:q * 64 + 64], a_nat[rows, j, 2, hd * 64:(hd + 1) * 64],
                                           a_xk[rows, j, hd, 0:64], start=False, stop=True)
                        fin(mm, ("H", j, s, c))

            def state(c, t, po):
                return a_h[po, t, 0, :] if c == 1 else a_s[po, c - 2, t, :]

            for c in range(1, 4):
                for e in range(2):
                    bank = start(("chain", c, e))
                    if c == 1:
                        for s in range(2):
                            for key in (("G", 1, s, 1), ("H", 1, s, 1)):
                                pe.wait_ge(*out(key))
                    else:
                        pe.wait_ge(*out(("chain", c - 1, e)))
                    po = halves(e)[1]
                    for t in range(4):
                        mm = pe.matmul(bank[po, t * 64:(t + 1) * 64], a_gt[po, t, c, :], state(c, t, po),
                                       start=True, stop=True)
                    fin(mm, ("chain", c, e))
            pe.wait_ge(*out(("Q1", 1, 1)))
            for q in range(2):
                for e in range(2):
                    bank = start(("OS", q, e))
                    po = halves(e)[1]
                    for t in (2 * q, 2 * q + 1):
                        for c in range(1, 4):
                            o = (t % 2) * SEQ + c * 64
                            mm = pe.matmul(bank[po, o:o + 64], state(c, t, po),
                                           kr[po, t, 1, c * 64:(c + 1) * 64], start=True, stop=True)
                    fin(mm, ("OS", q, e))

            J2 = slice(SEQ, T)
            for e in range(2):
                bank = start(("sgram", e))
                for t in range(4):
                    po = halves(e)[1]
                    pe.matmul(bank[NROW, t * P:t * P + 64], a_kk[po, t, J2], kr[po, t, :, J2], start=True, stop=True)
                    mm = pe.matmul(bank[NROW, t * P + 64:t * P + P], a_kt[po, t, J2], kr[po, t, :, J2],
                                   start=True, stop=True)
                fin(mm, ("sgram", e))
            for e in range(2):
                bank = start(("sgramL", e))
                for t in range(4):
                    po = halves(e)[1]
                    mm = pe.matmul(bank[NROW, t * NS:(t + 1) * NS], kr[po, t, 0, J2], a_kk[po, t, J2],
                                   start=True, stop=True)
                fin(mm, ("sgramL", e))
            bank = start(("sY", 0))
            pe.wait_ge(sem("s_masked"), 1)
            pe.wait_ge(sem("s_t0"), 1)
            for h in range(HA):
                mm = pe.matmul(bank[NROW, h * NS:(h + 1) * NS], s_a[:, h, :], s_t[:, h, :], start=True, stop=True)
            fin(mm, ("sY", 0))
            bank = start(("sXT", 0))
            pe.wait_ge(*out(("sY", 0)))
            for h in range(HA):
                mm = pe.matmul(bank[NROW, h * NS:(h + 1) * NS], s_y[:, h, :], s_tt[:, h, :], start=True, stop=True)
            fin(mm, ("sXT", 0))
            bank = start(("sMV", 0))
            for h in range(HA):
                mm = pe.matmul(bank[NROW, h * 64:(h + 1) * 64], s_at[:, h, 64:96],
                               a_nat[NROW, 2, 0, h * 64:(h + 1) * 64], start=True, stop=True)
            fin(mm, ("sMV", 0))
            pe.wait_ge(sem("s_kb"), 1)
            pe.wait_ge(sem("rwkv_in"), 16)
            for e in range(2):
                bank = start(("sX", e))
                for t in range(4):
                    po = halves(e)[1]
                    for b in range(DB):
                        mm = pe.matmul(bank[NROW, t * 64:(t + 1) * 64], a_kb[po, t, b * 64:b * 64 + NS],
                                       a_s0[po, t, b, :], start=(b == 0), stop=(b == DB - 1))
                fin(mm, ("sX", e))
            bank = start(("sU", 0))
            pe.wait_ge(*out(("sX", 0)))
            pe.wait_ge(*out(("sX", 1)))
            pe.wait_ge(*out(("sXT", 0)))
            for h in range(HA):
                mm = pe.matmul(bank[NROW, h * 64:(h + 1) * 64], s_tt[:, h, :], s_x[:, h, :], start=True, stop=True)
            fin(mm, ("sU", 0))
            bank = start(("sO", 0))
            pe.wait_ge(*out(("sU", 0)))
            for h in range(HA):
                t, po = halves(h)
                pe.matmul(bank[po, t * NS:(t + 1) * NS], a_nat[NROW, 2, 0, h * 64:(h + 1) * 64],
                          s_at[:, h, 96:128], start=True, stop=False)
                mm = pe.matmul(bank[po, t * NS:(t + 1) * NS], s_u[:, h, :], s_at[:, h, 32:64],
                               start=False, stop=True)
            fin(mm, ("sO", 0))
            for e in range(2):
                bank = start(("sOS", e))
                for t in range(4):
                    po = halves(e)[1]
                    for b in range(DB):
                        mm = pe.matmul(bank[po, t * NS + 4 * b:t * NS + 4 * b + 4], a_s0[po, t, b, :],
                                       kr[po, t, 1, SEQ + 4 * b:SEQ + 4 * b + 4], start=True, stop=True)
                fin(mm, ("sOS", e))
            pe.wait_ge(sem("s_vb"), 2)
            for t in range(4):
                bank = start(("sS", t))
                for h in (2 * t, 2 * t + 1):
                    po = halves(h)[1]
                    pe.matmul(bank[po, 0:512], a_nat[NROW, 2, 1, h * 64:(h + 1) * 64],
                              s_vb[:, h, :, :], start=True, stop=False)
                    mm = pe.matmul(bank[po, 0:512], a_nat[NROW, 2, 2, h * 64:(h + 1) * 64],
                                   s_ub[:, h, :, :], start=False, stop=True)
                fin(mm, ("sS", t))
            for k in (("OS", 1, 0), ("OS", 1, 1), ("sOS", 0), ("sOS", 1)):
                pe.wait_ge(*out(k))

            def head_sums(key, src):
                for t in range(4):
                    bank = start((key, t))
                    fin(pe.matmul(bank[:, 0:T], C("blk"), src[:, t, :], start=True, stop=True), (key, t))

            def by_token(key, t0, j):
                bank = start((key, j))
                for h in range(4):
                    mm = pe.transpose(bank[0:P if j < 2 else NS, h * P:(h + 1) * P], b_z[:, t0 + h, tok(j)], C("ident"))
                fin(mm, (key, j))

            def scores(j):
                rows, cols = (slice(0, P), P) if j < 2 else (NROW, NS)
                key = ("ratt", j) if j < 2 else ("rsatt", 0)
                bank = start(key)
                for h in range(4):
                    mm = pe.matmul(bank[rows, h * cols:(h + 1) * cols], b_z[:, 4 + h, tok(j)], b_z[:, h, tok(j)],
                                   start=True, stop=True)
                fin(mm, key)

            def from_state(h):
                bank = start(("rQ", h))
                for b in range(DB):
                    mm = pe.matmul(bank[:, 4 * b:4 * b + 4], b_s0[:, h, b, :], b_qx[:, h, SEQ + 4 * b:SEQ + 4 * b + 4],
                                   start=True, stop=True)
                fin(mm, ("rQ", h))

            zb_use = TABLE["zb"][3]

            def behind_zb(k):
                if k == 0:
                    pe.wait_ge(sem("gn_sq"), 1)
                    head_sums("gnv", a_kk)
                elif 2 <= k <= 9:
                    t = k - 2
                    pe.wait_ge(bank_free[t % 4], zb_use[t % 4] + t // 4 + 1)
                    bank = start(("rot", t))
                    fin(pe.matmul(bank[:, 0:T], C("rot"), b_z[:, t, :], start=True, stop=True), ("rot", t))
                elif k == 11:
                    pe.wait_ge(sem("rotated"), 8)
                    by_token("rkn", 4, 0)
                elif k == 12:
                    by_token("rkn", 4, 1)
                    by_token("rkn", 4, 2)
                    pe.wait_ge(sem("qx"), 1)
                    pe.wait_ge(sem("ret_in"), 16)
                    from_state(0)
                elif k == 13:
                    pe.wait_ge(bank_free[3], zb_use[3] + 3)
                    for b in range(3):
                        pe.wait_ge(bank_free[b], zb_use[b] + 3)
                    by_token("rvn", 8, 0)
                    by_token("rvn", 8, 1)
                    from_state(1)
                elif k == 14:
                    by_token("rvn", 8, 2)
                    scores(0)
                    from_state(2)
                elif k == 15:
                    scores(1)
                    from_state(3)

            head_sums("gnm", a_ld)
            stage("zb", 1, behind_zb)
            scores(2)
            for j in range(2):
                bank = start(("rS", j))
                pe.wait_ge(*out(("rvn", j)))
                pe.wait_ge(*out(("rkn", j)))
                for h in range(4):
                    mm = pe.matmul(bank[:, h * P:(h + 1) * P], b_kz[:, j, h, :], b_vn[:, j, h, :],
                                   start=True, stop=True)
                fin(mm, ("rS", j))
            pe.wait_ge(*out(("ratt", 1)))
            pe.wait_ge(*out(("rsatt", 0)))
            pe.wait_ge(*out(("rvn", 2)))
            pe.wait_ge(*out(("rS", 0)))

            def ret_out(h):
                bank = start(("rO", h))
                pe.matmul(bank[:, 0:P], b_vn[:, 0, h, :], b_at[:, 0, h, :], start=True, stop=True)
                pe.matmul(bank[:, P:2 * P], b_vn[:, 1, h, :], b_at[:, 1, h, :], start=True, stop=False)
                pe.matmul(bank[:, P:2 * P], b_s[:, 0, h, :], b_qx[:, h, P:2 * P], start=False, stop=True)
                fin(pe.matmul(bank[:, SEQ:T], b_vn[NROW, 2, h, :], b_sat[:, h, :], start=True, stop=True), ("rO", h))

            def ret_sum(key, h):
                if key == "rgm":
                    pe.wait_ge(*out(("rO", h)))
                else:
                    pe.wait_ge(sem("rg_sq"), h + 1)
                bank = start((key, h))
                src = b_ot if key == "rgm" else b_qx
                fin(pe.matmul(bank[:, 0:T], C("ones"), src[:, h, :], start=True, stop=True), (key, h))

            ret_out(0)
            ret_out(1)
            ret_sum("rgm", 0)
            ret_out(2)
            ret_sum("rgm", 1)
            ret_sum("rgv", 0)
            ret_out(3)
            ret_sum("rgm", 2)
            ret_sum("rgv", 1)
            ret_sum("rgm", 3)
            ret_sum("rgv", 2)
            ret_sum("rgv", 3)

            def behind_abo(k):
                if k == 0:
                    pe.wait_ge(*out(("rkn", 2)))
                    pe.wait_ge(sem("b_vb"), 1)
                if k < 4:
                    for q in range(2):
                        bank = start(("rsS", k, q))
                        fin(pe.matmul(bank[:, 0:512], b_kz[NROW, 2, k, :], b_vb[:, k, 4 * q:4 * q + 4, :],
                                      start=True, stop=True), ("rsS", k, q))

            stage("abo", 2, behind_abo)

        def invert_tensor(pe, start, fin, tag, j, tm, tt, ym, am):
            for l in range(1, LEVELS):
                for s in range(2):
                    key = ("Y", tag, j, s, l)
                    bank = start(key)
                    pe.wait_ge(sem("masked"), masked_count(j, s, l))
                    if l == 1:
                        pe.wait_ge(sem("t0"), 2 * j + s + 1)
                    else:
                        pe.wait_ge(*out(("X", tag, j, s, l - 1)))
                    for h in range(4):
                        mm = pe.matmul(bank[:, h * P:(h + 1) * P], am[s][:, h, :], tm[s][:, h, :],
                                       start=True, stop=True)
                    fin(mm, key)
                for s in range(2):
                    if l == 1:
                        pe.wait_ge(sem("tt0"), 2 * j + s + 1)
                    else:
                        pe.wait_ge(*out(("XT", tag, j, s, l - 1)))
                    pe.wait_ge(*out(("Y", tag, j, s, l)))
                    for name in ("X", "XT")[(0 if l < LEVELS - 1 else 1):]:
                        key = (name, tag, j, s, l)
                        bank = start(key)
                        for h in range(4):
                            lhs, rhs = (tt, ym) if name == "X" else (ym, tt)
                            mm = pe.matmul(bank[:, h * P:(h + 1) * P], lhs[s][:, h, :], rhs[s][:, h, :],
                                           start=True, stop=True)
                        fin(mm, key)

        def ab_scalar(act, env):
            link = env["link"]

            def jb(key, w=512):
                return jobb[bank_of(key)][:, 0:w]

            def copy(key, dst, src, scale=1.0):
                nc.scalar.activation(dst, src, ACT.Copy, scale=scale).then_inc(drained[bank_of(key)], 1)

            def rows_in(i, j, u0, use):
                k = 4 * i + j
                t = ZA_ORDER[k]
                if k == 0:
                    act.wait_ge(sem("shift_pad"), 1)
                act.wait_ge(unit_done, u0 + k + 1)
                nc.scalar.activation(a_zp[:, t, 1:1 + SEQ], gemm[j][:, 0:SEQ], ACT.Copy)
                nc.scalar.activation(a_zp[:, t, 1 + SEQ:ZPW].rearrange("p (b s) -> p b s", s=5)[:, :, 1:5],
                                     gemm[j][:, SEQ:T].rearrange("p (b s) -> p b s", s=DS), ACT.Copy
                                     ).then_inc(bank_free[j], 1)
                if k == 3:
                    act.wait_ge(sem("shifted"), 2)
                    nc.scalar.activation(a_z[0:64, 12, :], a_z[0:64, 12, :], ACT.Tanh).then_inc(sem("lora_act"), 1)
                    nc.scalar.activation(a_z[:, 13, :], a_z[:, 13, :], ACT.Sigmoid).then_inc(sem("lora_act"), 1)
                elif k in (4, 5, 6):
                    name, dst, bias = (("lora_w", a_ld, "w0"), ("lora_a", a_a, "a0"), ("gate", a_gate, None))[k - 4]
                    for t in range(4):
                        act.wait_ge(*full((name, t)))
                        src = jb((name, t), T)
                        if bias:
                            nc.scalar.activation(dst[:, t, :], src, ACT.Sigmoid, bias=pc(bias, t)
                                                 ).then_inc(drained[bank_of((name, t))], 1)
                        else:
                            copy((name, t), dst[:, t, :], src)
                elif k == 9:
                    act.wait_ge(*out(("l2", 3)))
                    link(nc.scalar.activation(m(A_TB, 1152), m(A_TB, 1152), ACT.Ln))
                elif k == 10:
                    nc.scalar.activation(m(A_TB, 1152), m(A_TB, 1152), ACT.Exp, scale=-0.5).then_inc(sem("knorm"), 1)
                elif k == 11:
                    act.wait_ge(sem("cums"), 1)
                    nc.scalar.activation(m(A_EIN, 1152), m(A_CUM, 1152), ACT.Exp).then_inc(sem("ein"), 1)
                elif k == 12:
                    nc.scalar.activation(m(A_LD, 1152), m(A_LD, 1152), ACT.Exp).then_inc(sem("eld"), 1)

            env["stage"]("za", rows_in)
            act.wait_ge(sem("ein"), 1)
            nc.scalar.activation(m(A_CUM, 1152), m(A_CUM, 1152), ACT.Exp, scale=-1.0).then_inc(sem("ecum"), 1)
            nc.scalar.activation(m(A_EE, 1152), m(A_EE, 1152), ACT.Exp).then_inc(sem("exps"), 1)
            act.wait_ge(sem("last_rows"), 1)
            for mt in NAT_ORDER[:3]:
                for j in range(3):
                    w = P if j < 2 else NS
                    key = ("nat", j, mt)
                    act.wait_ge(*full(key))
                    if mt == 3:
                        copy(key, a_xk[0:w, j, :, 64:128], jb(key)[0:w].rearrange("p (h k) -> p h k", h=8))
                    else:
                        copy(key, a_nat[0:w, j, mt, :], jb(key)[0:w])
            for j in range(2):
                for s in range(2):
                    act.wait_ge(*full(("MV", j, s)))
                    key = ("MV", j, s)
                    copy(key, a_xk[:, j, 4 * s:4 * s + 4, 0:64],
                         jb(key, 256).rearrange("p (h v) -> p h v", h=4))
                invert_scalar(act, "a", j, YM)
                for s in range(2):
                    key = ("UW", j, s)
                    act.wait_ge(*full(key))
                    copy(key, a_xk[:, j, 4 * s:4 * s + 4, :], jb(key).rearrange("p (h v) -> p h v", h=4), -1.0)
                    for c in range(2):
                        key = ("H", j, s, c)
                        act.wait_ge(*full(key))
                        copy(key, a_h[:, 2 * s:2 * s + 2, 2 * j + c, :],
                             jb(key, P).rearrange("p (t v) -> p t v", t=2))
            key = ("sY", 0)
            act.wait_ge(*full(key))
            copy(key, s_y, jb(key, 256)[NROW].rearrange("p (h t) -> p h t", h=8))
            for key, dst, sc in ((("sMV", 0), s_x, 1.0), (("sU", 0), s_u, -1.0)):
                act.wait_ge(*full(key))
                copy(key, dst, jb(key)[NROW].rearrange("p (h t) -> p h t", h=8), sc)
            act.wait_ge(*out(("gnm", 3)))
            nc.scalar.activation(m(A_KK, 1152), m(A_LD, 1152), ACT.Square).then_inc(sem("gn_sq"), 1)

            def between_zb(i, j, u0, use):
                k = 4 * i + j
                if k >= 12:
                    act.wait_ge(unit_done, u0 + k + 1)
                    nc.scalar.activation(b_z[:, k, :], gemm[j][:, 0:T], ACT.Silu).then_inc(bank_free[j], 1)
                if k == 1:
                    for t in range(4):
                        key = ("gnv", t)
                        act.wait_ge(*full(key))
                        nc.scalar.activation(a_rs[:, t, :], jb(key, T), ACT.Ln, bias=C("eps")[:, 2:3], scale=1.0 / 64
                                             ).then_inc(drained[bank_of(key)], 1)
                elif k == 2:
                    act.wait_ge(*out(("gnv", 3)))
                    nc.scalar.activation(a_rs, a_rs, ACT.Exp, scale=-0.5).then_inc(sem("gn_rstd"), 1)
                elif k >= 13:
                    key = ("rQ", k - 13)
                    act.wait_ge(*full(key))
                    copy(key, b_ot[:, k - 13, SEQ:T], jb(key, NS))
                    for q in ((), (0, 1), (2,))[k - 13]:
                        w = P if q < 2 else NS
                        key = ("rvn", q)
                        act.wait_ge(*full(key))
                        copy(key, b_vn[0:w, q, :, :], jb(key)[0:w].rearrange("p (h v) -> p h v", h=4))

            act.wait_ge(sem("stored"), 48)
            env["stage"]("zb", between_zb)
            key = ("rQ", 3)
            act.wait_ge(*full(key))
            copy(key, b_ot[:, 3, SEQ:T], jb(key, NS))
            key = ("rS", 0)
            act.wait_ge(*full(key))
            copy(key, b_s[:, 0, :, :], jb(key).rearrange("p (h v) -> p h v", h=4))

            def ret_copy(h):
                key = ("rO", h)
                act.wait_ge(sem("rq_added"), h + 1)
                copy(key, b_ot[:, h, 0:SEQ], jb(key, SEQ))

            def ret_square(h):
                act.wait_ge(*out(("rgm", h)))
                nc.scalar.activation(b_qx[:, h, :], b_ot[:, h, :], ACT.Square).then_inc(sem("rg_sq"), 1)

            def ret_ln(h):
                key = ("rgv", h)
                act.wait_ge(*full(key))
                nc.scalar.activation(b_rt[:, h, :], jb(key, T), ACT.Ln, bias=C("eps")[:, 3:4], scale=1.0 / P
                                     ).then_inc(drained[bank_of(key)], 1)

            for step, h in ((ret_copy, 0), (ret_copy, 1), (ret_square, 0), (ret_copy, 2), (ret_square, 1), (ret_ln, 0),
                            (ret_copy, 3), (ret_square, 2), (ret_ln, 1), (ret_square, 3), (ret_ln, 2), (ret_ln, 3)):
                step(h)
            act.wait_ge(*out(("rgv", 3)))
            nc.scalar.activation(r[:, 0:1152], r[:, 0:1152], ACT.Exp, scale=-0.5).then_inc(sem("rg_rstd"), 1)
            act.wait_ge(sem("y_rwkv"), 1)
            for d in range(DT):
                if d >= 4:
                    act.wait_ge(sem("y_ret"), d - 3)
                src = a_gate[:, d, :] if d < 4 else b_ot[:, d - 4, :]
                nc.scalar.activation(xhi[:, d, :], src, ACT.Copy).then_inc(x_hi, 1)
            env["stage"]("abo", env["idle"])

        def invert_scalar(act, tag, j, ym):
            for l in range(1, LEVELS):
                for s in range(2):
                    key = ("Y", tag, j, s, l)
                    act.wait_ge(*full(key))
                    nc.scalar.activation(ym[s], jobb[bank_of(key)][:].rearrange("p (h t) -> p h t", h=4),
                                         ACT.Copy).then_inc(drained[bank_of(key)], 1)

        def ab_vector(dve, env):
            link = env["link"]
            V = nc.vector

            def jb(key, w=512):
                return jobb[bank_of(key)][:, 0:w]

            def read(ins, key):
                ins.then_inc(drained[bank_of(key)], 1)

            def shift(i, j, u0, use):
                k = 4 * i + j
                t = ZA_ORDER[k]
                dve.wait_ge(bank_free[j], use[j] + i + 1)
                d, z = a_dz[:, k % 2, :], a_zp[:, t, :]
                link(V.tensor_tensor(d[:, 0:ZPW - 1], z[:, 0:ZPW - 1], z[:, 1:ZPW], ALU.subtract))
                V.scalar_tensor_tensor(out=a_z[:, t, 0:SEQ], in0=d[:, 0:SEQ], scalar=pc("mu", t), in1=z[:, 1:1 + SEQ],
                                       op0=ALU.mult, op1=ALU.add)
                V.scalar_tensor_tensor(out=a_z[:, t, SEQ:T].rearrange("p (b s) -> p b s", s=DS),
                                       in0=d[:, 1 + SEQ:ZPW].rearrange("p (b s) -> p b s", s=5)[:, :, 0:4],
                                       scalar=pc("mu", t),
                                       in1=z[:, 1 + SEQ:ZPW].rearrange("p (b s) -> p b s", s=5)[:, :, 1:5],
                                       op0=ALU.mult, op1=ALU.add).then_inc(sem("shifted"), 1)
                if k == 5:
                    dve.wait_ge(sem("shifted"), 6)
                    for t in range(4):
                        ins = V.tensor_scalar(a_kk[:, t, :], a_z[:, 4 + t, :], pc("kk", t), None, ALU.mult)
                    ins.then_inc(sem("kk"), 1)
                elif k == 6:
                    dve.wait_ge(sem("kk"), 1)
                    V.tensor_tensor(m(A_TB, 1152), m(A_KK, 1152), m(A_KK, 1152), ALU.mult).then_inc(sem("ksq"), 1)
                elif k == 7:
                    dve.wait_ge(*out(("lora_w", 3)))
                    link(V.tensor_scalar(m(A_LD, 1152), m(A_LD, 1152), -EM05, None, ALU.mult))
                    for t in range(4):
                        ins = V.tensor_tensor_scan(out=a_cum[:, t, :], data0=C("scan"), data1=a_ld[:, t, :],
                                                   initial=0.0, op0=ALU.mult, op1=ALU.add)
                    link(ins)
                elif k == 8:
                    for t in range(4):
                        dve.wait_ge(*full(("l2", t)))
                        read(V.tensor_scalar(a_tb[:, t, :], jb(("l2", t), T), 1e-12, None, ALU.max), ("l2", t))
                elif k == 9:
                    V.tensor_tensor(m(A_LD, 1152), m(A_CUM, 1152), m(A_LD, 1152), ALU.subtract)
                elif k == 10:
                    cp = a_cum[:, :, 0:SEQ].rearrange("p t (c s) -> p t c s", s=CH)
                    ep = a_ee[:, :, 0:SEQ].rearrange("p t (c s) -> p t c s", s=CH)
                    cs = a_cum[:, :, SEQ:T].rearrange("p t (c s) -> p t c s", s=DS)
                    es = a_ee[:, :, SEQ:T].rearrange("p t (c s) -> p t c s", s=DS)
                    V.tensor_tensor(ep, cp[:, :, :, CH - 1:CH].to_broadcast([P, 4, 4, CH]), cp, ALU.subtract)
                    V.tensor_tensor(es, cs[:, :, :, DS - 1:DS].to_broadcast([P, 4, DB, DS]), cs,
                                    ALU.subtract).then_inc(sem("cums"), 1)
                elif k == 11:
                    dve.wait_ge(sem("knorm"), 1)
                    link(V.tensor_tensor(m(A_KK, 1152), m(A_KK, 1152), m(A_TB, 1152), ALU.mult))
                elif k == 12:
                    dve.wait_ge(sem("k_scaled"), 1)
                    link(V.tensor_tensor(m(A_A, 1152), m(A_A, 1152), m(A_KK, 1152), ALU.mult))

            dve.wait_ge(sem("shift_pad"), 1)
            env["stage"]("za", shift)
            dve.wait_ge(sem("shifted"), 14)
            for t in range(4):
                dve.wait_ge(*full(("bonus", t)))
                read(V.tensor_tensor(a_tb[:, t, :], a_z[:, 8 + t, :], jb(("bonus", t), T), ALU.mult), ("bonus", t))
            dve.wait_ge(sem("eld"), 1)
            V.tensor_tensor(kr[:, :, 0, :], a_kk, a_ld, ALU.mult).then_inc(sem("kk_prev"), 1)
            dve.wait_ge(sem("kk_prev"), 1)
            dve.wait_ge(sem("ecum"), 1)
            V.tensor_tensor(m(A_KK, 1152), m(A_A, 1152), m(A_CUM, 1152), ALU.mult).then_inc(sem("a_used"), 1)
            dve.wait_ge(sem("rp"), 1)
            link(V.tensor_tensor(m(A_KT, 1152), m(A_Z + 4 * T, 1152), m(A_CUM, 1152), ALU.mult))
            dve.wait_ge(sem("exps"), 1)
            V.tensor_tensor(m(A_Z + 4 * T, 1152), m(A_Z + 4 * T, 1152), m(A_EE, 1152), ALU.mult)
            V.tensor_copy(a_pc[:, :, 0:4], a_ein[:, :, CH - 1:SEQ:CH])
            V.tensor_copy(a_pc[:, :, 4:12], a_ein[:, :, SEQ + DS - 1:T:DS]).then_inc(sem("operands"), 1)
            for j in range(3):
                w = P if j < 2 else NS
                key = ("nat", j, 2)
                dve.wait_ge(*full(key))
                read(V.tensor_copy(a_nat[0:w, j, 2, :], jb(key)[0:w]), key)
            dve.wait_ge(sem("operands"), 1)
            for j in range(2):
                for s in range(2):
                    for h in range(4):
                        key = ("gram", j, s, h)
                        dve.wait_ge(*full(key))
                        read(V.tensor_tensor(AT[s][:, h, :].rearrange("p (x c) -> p x c", x=2),
                                             jb(key).rearrange("p (x c) -> p x c", x=2),
                                             bc(C("up64"), 1, 2), ALU.mult), key)
                    for e in range(2):
                        key = ("gramL", j, s, e)
                        dve.wait_ge(*full(key))
                        read(V.tensor_tensor(TM[s][:, e::2, :], jb(key, 256).rearrange("p (h t) -> p h t", h=2),
                                             bc(C("low0"), 1, 2), ALU.mult), key)
                        dve.wait_ge(*out(key))
                    V.tensor_tensor(TM[s], mask4("ident", P), TM[s], ALU.subtract).then_inc(sem("t0"), 1)
                    link(V.tensor_tensor(TT[s], AT[s][:, :, 0:P], mask4("lev0", P), ALU.mult))
                    V.tensor_tensor(TT[s], mask4("ident", P), TT[s], ALU.subtract).then_inc(sem("tt0"), 1)
                invert_vector(dve, "a", j, TM, TT)
                for s in range(2):
                    key = ("O0", j, s)
                    dve.wait_ge(*full(key))
                    read(V.tensor_copy(a_ld[:, 2 * s:2 * s + 2, tok(j)],
                                       jb(key, 256).rearrange("p (t c) -> p t c", t=2)), key)
                    key = ("Q1", j, s)
                    dve.wait_ge(*full(key))
                    o = kr[:, 2 * s:2 * s + 2, 1, tok(j)]
                    read(V.tensor_tensor(o, jb(key, 256).rearrange("p (t c) -> p t c", t=2), o, ALU.add), key)
                    for c in range(2):
                        key = ("G", j, s, c)
                        dve.wait_ge(*full(key))
                        for q in range(2):
                            t, ck = 2 * s + q, 2 * j + c
                            ins = V.scalar_tensor_tensor(out=a_gt[:, t, ck, :], in0=C("id64"),
                                                         scalar=a_pc[:, t, ck:ck + 1],
                                                         in1=jobb[bank_of(key)][:, q * 64:q * 64 + 64],
                                                         op0=ALU.mult, op1=ALU.add)
                        read(ins, key)
            for j in range(2):
                for s in range(2):
                    for c in range(2):
                        dve.wait_ge(*out(("H", j, s, c)))
            for c in range(1, 4):
                for e in range(2):
                    key = ("chain", c, e)
                    po = halves(e)[1]
                    dve.wait_ge(*full(key))
                    read(V.tensor_tensor(a_s[po, c - 1, :, :], jb(key, 256)[po].rearrange("p (t v) -> p t v", t=4),
                                         a_h[po, :, c, :], ALU.add), key)
            dve.wait_ge(*out(("O0", 1, 1)))
            for q in range(2):
                for e in range(2):
                    key = ("OS", q, e)
                    po = halves(e)[1]
                    dve.wait_ge(*full(key))
                    o = a_ld[po, 2 * q:2 * q + 2, CH:SEQ]
                    read(V.tensor_tensor(o, jb(key)[po].rearrange("p (t c) -> p t c", t=2)[:, :, CH:SEQ], o,
                                         ALU.add), key)
            for e in range(2):
                key = ("sgram", e)
                dve.wait_ge(*full(key))
                o = s_at[:, e::2, :].rearrange("p h (x c) -> p h x c", x=2)
                src = jb(key)[NROW].rearrange("p (h x c) -> p h x c", h=4, x=2)
                for xx in range(2):
                    ins = V.tensor_tensor(o[:, :, xx, :], src[:, :, xx, :], mask4("up4", 64, NROW), ALU.mult)
                read(ins, key)
            for e in range(2):
                key = ("sgramL", e)
                dve.wait_ge(*full(key))
                read(V.tensor_tensor(s_t[:, e::2, :], jb(key, P)[NROW].rearrange("p (h t) -> p h t", h=4),
                                     bc(C("low0", NROW)[:, 0:NS], 1, 4), ALU.mult), key)
                dve.wait_ge(*out(key))
            V.tensor_tensor(s_t, bc(C("ident", NROW)[:, 0:NS], 1, 8), s_t, ALU.subtract).then_inc(sem("s_t0"), 1)
            key = ("sXT", 0)
            dve.wait_ge(*full(key))
            dve.wait_ge(sem("s_masked"), 1)
            read(V.tensor_tensor(s_tt, s_tt, jb(key, 256)[NROW].rearrange("p (h t) -> p h t", h=8),
                                 ALU.subtract), key)
            dve.wait_ge(*out(("sMV", 0)))
            for e in range(2):
                key = ("sX", e)
                dve.wait_ge(*full(key))
                read(V.tensor_tensor(s_x[:, e::2, :], s_x[:, e::2, :],
                                     jb(key, 256)[NROW].rearrange("p (h v) -> p h v", h=4), ALU.add), key)
            dve.wait_ge(*out(("sU", 0)))
            selb = C("selb", NROW)
            V.tensor_tensor(s_ub, bc(s_u, 2, DB), bc(bc(selb, 1, 8), 3, 64), ALU.mult).then_inc(sem("s_vb"), 1)
            key = ("sO", 0)
            dve.wait_ge(*full(key))
            read(V.tensor_copy(a_ld[:, :, SEQ:T], jb(key, P).rearrange("p (t c) -> p t c", t=4)), key)
            dve.wait_ge(*out(key))
            for e in range(2):
                key = ("sOS", e)
                po = halves(e)[1]
                dve.wait_ge(*full(key))
                read(V.tensor_tensor(a_ld[po, :, SEQ:T], jb(key, P)[po].rearrange("p (t c) -> p t c", t=4),
                                     a_ld[po, :, SEQ:T], ALU.add), key)
            for t in range(4):
                key = ("sS", t)
                dve.wait_ge(*full(key))
                link(V.tensor_tensor(a_s0[:, t, :, :], a_s0[:, t, :, :], bc(a_pc[:, t, 4:12], 2, 64), ALU.mult))
                read(V.tensor_tensor(a_s0[:, t, :, :], a_s0[:, t, :, :],
                                     jb(key).rearrange("p (b v) -> p b v", b=8), ALU.add), key)
            dve.wait_ge(*out(("sOS", 1)))
            dve.wait_ge(*out(("OS", 1, 1)))
            for t in range(4):
                key = ("gnm", t)
                dve.wait_ge(*full(key))
                read(V.scalar_tensor_tensor(out=a_ld[:, t, :], in0=jb(key, T), scalar=-1.0 / 64, in1=a_ld[:, t, :],
                                            op0=ALU.mult, op1=ALU.add), key)
            def between_zb(i, j, u0, use):
                k = 4 * i + j
                if k < 12:
                    dve.wait_ge(unit_done, u0 + k + 1)
                    V.tensor_copy(b_z[:, k, :], gemm[j][:, 0:T]).then_inc(bank_free[j], 1)
                if k == 2:
                    dve.wait_ge(sem("gn_rstd"), 1)
                    for t in range(4):
                        V.scalar_tensor_tensor(out=a_ld[:, t, :], in0=a_ld[:, t, :], scalar=pc("gng", t),
                                               in1=a_rs[:, t, :], op0=ALU.mult, op1=ALU.mult
                                               ).then_inc(sem("gn_scaled"), 1)
                    for t in range(4):
                        dve.wait_ge(sem("gn_scaled"), t + 1)
                        V.scalar_tensor_tensor(out=a_ld[:, t, :], in0=a_ld[:, t, :], scalar=pc("gnb", t),
                                               in1=a_tb[:, t, :], op0=ALU.add, op1=ALU.add
                                               ).then_inc(sem("gn_done"), 1)
                if 3 <= k <= 10:
                    t = k - 3
                    key = ("rot", t)
                    dve.wait_ge(*full(key))
                    read(V.tensor_tensor(b_rt[:, t, :], jb(key, T), C("sin"), ALU.mult), key)
                    dve.wait_ge(*out(key))
                    dve.wait_ge(sem("cosine"), t + 1)
                    V.tensor_tensor(b_z[:, t, :], b_z[:, t, :], b_rt[:, t, :], ALU.add).then_inc(sem("rotated"), 1)
                elif k == 11:
                    dve.wait_ge(sem("rotated"), 8)
                    for q in range(2):
                        V.tensor_tensor(b_qx[:, :, tok(q)], b_z[:, 0:4, tok(q)],
                                        C("xi").rearrange("p (h t) -> p h t", h=4), ALU.mult)
                    V.tensor_tensor(b_qx[:, :, SEQ:T], b_z[:, 0:4, SEQ:T],
                                    C("xi4").rearrange("p (h t) -> p h t", h=4), ALU.mult).then_inc(sem("qx"), 1)
                elif k in (12, 13):
                    for q in ((0,) if k == 12 else (1, 2)):
                        w = slice(0, P if q < 2 else NS)
                        key = ("rkn", q)
                        dve.wait_ge(*full(key))
                        read(V.scalar_tensor_tensor(out=b_kz[w, q, :, :], in0=jb(key)[w].rearrange(
                            "p (h k) -> p h k", h=4), scalar=QSCALE, in1=bc(C("zeta" if q < 2 else "zeta4", w), 2, P),
                            op0=ALU.mult, op1=ALU.mult), key)
                elif k == 15:
                    decayed(0)

            def decayed(j):
                if j < 2:
                    key, dst, src, dec = ("ratt", j), b_at[:, j, :, :], jb(("ratt", j)), C("rdec")
                else:
                    key = ("rsatt", 0)
                    dst, src, dec = b_sat, jb(key, P)[NROW], C("rdec4", NROW)
                dve.wait_ge(*full(key))
                read(V.scalar_tensor_tensor(out=dst, in0=src.rearrange("p (h t) -> p h t", h=4), scalar=QSCALE,
                                            in1=dec.rearrange("p (h t) -> p h t", h=4), op0=ALU.mult,
                                            op1=ALU.mult), key)

            dve.wait_ge(sem("stored"), 48)
            env["stage"]("zb", between_zb)
            decayed(1)
            decayed(2)
            key = ("rS", 1)
            dve.wait_ge(*full(key))
            dve.wait_ge(*out(("rS", 0)))
            for h in range(4):
                ins = V.scalar_tensor_tensor(out=b_s[:, 1, h, :], in0=b_s[:, 0, h, :], scalar=GAMMA[h] ** P,
                                             in1=jobb[bank_of(key)][:, h * P:(h + 1) * P],
                                             op0=ALU.mult, op1=ALU.add)
            read(ins, key)

            def sample_part(h):
                key = ("rO", h)
                dve.wait_ge(*out(("rQ", h)))
                dve.wait_ge(*full(key))
                o = b_ot[:, h, SEQ:T]
                V.tensor_tensor(o, o, jb(key, T)[:, SEQ:T], ALU.add).then_inc(sem("rq_added"), 1)

            sample_part(0)
            sample_part(1)
            for h in range(4):
                if h < 2:
                    sample_part(h + 2)
                key = ("rgm", h)
                dve.wait_ge(*full(key))
                read(V.scalar_tensor_tensor(out=b_ot[:, h, :], in0=jb(key, T), scalar=-1.0 / P, in1=b_ot[:, h, :],
                                            op0=ALU.mult, op1=ALU.add), key)
            dve.wait_ge(sem("rg_rstd"), 1)
            for h in range(4):
                V.scalar_tensor_tensor(out=b_ot[:, h, :], in0=b_ot[:, h, :], scalar=pc("rgg", h), in1=b_rt[:, h, :],
                                       op0=ALU.mult, op1=ALU.mult).then_inc(sem("rg_scaled"), 1)
            for h in range(4):
                dve.wait_ge(sem("rg_scaled"), h + 1)
                V.scalar_tensor_tensor(out=b_ot[:, h, :], in0=b_ot[:, h, :], scalar=pc("rgb", h), in1=b_z[:, 12 + h, :],
                                       op0=ALU.add, op1=ALU.mult).then_inc(sem("y_ret"), 1)
            low_parts(dve, V, 2, 0, lambda d: a_gate[:, d, :] if d < 4 else b_ot[:, d - 4, :])
            to_residual = env["residual"](ALPHA, "out")

            def between_abo(i, j, u0, use):
                k = 4 * i + j
                to_residual(i, j, u0, use)
                if 1 <= k <= 4:
                    h = k - 1
                    for q in range(2):
                        key = ("rsS", h, q)
                        dve.wait_ge(*full(key))
                        o = b_s0[:, h, 4 * q:4 * q + 4, :]
                        read(V.scalar_tensor_tensor(out=o, in0=o, scalar=GAMMA[h] ** DS,
                                                    in1=jb(key).rearrange("p (b v) -> p b v", b=4),
                                                    op0=ALU.mult, op1=ALU.add), key)

            env["stage"]("abo", between_abo)

        def invert_vector(dve, tag, j, tm, tt):
            for l in range(1, LEVELS):
                for s in range(2):
                    for name, dst in (("X", tm), ("XT", tt))[(0 if l < LEVELS - 1 else 1):]:
                        key = (name, tag, j, s, l)
                        dve.wait_ge(*full(key))
                        nc.vector.tensor_tensor(dst[s], dst[s],
                                                jobb[bank_of(key)][:].rearrange("p (h t) -> p h t", h=4),
                                                ALU.subtract).then_inc(drained[bank_of(key)], 1)

        def ab_pool(pool, env):
            link = env["link"]
            G = nc.gpsimd
            pool.dma_start(a_sh, a["shift_in"]).then_inc(sem("shift_in"), 16)
            G.memset(a_zp[:, :, 0:1], 0.0)
            pool.wait_ge(sem("shift_in"), 16)
            G.tensor_copy(a_zp[:, :, 1 + SEQ:ZPW].rearrange("p t (b s) -> p t b s", s=5)[:, :, :, 0], a_sh
                          ).then_inc(sem("shift_pad"), 1)
            at = PCOLS["ka"][0]
            link(G.tensor_scalar(a_km, par[:, at:at + 4], 1.0, None, ALU.subtract))
            pool.wait_ge(*out(("lora_a", 3)))
            for t in range(4):
                ins = G.tensor_scalar(a_k1[:, t, :], a_a[:, t, :], pc("ka", t), a_km[:, t:t + 1], ALU.mult,
                                      ALU.subtract)
            link(ins)
            pool.wait_ge(sem("kk"), 1)
            G.tensor_tensor(a_z[:, 4:8, :], a_k1, a_z[:, 4:8, :], ALU.mult).then_inc(sem("k_scaled"), 1)
            pool.wait_ge(sem("k_scaled"), 1)
            pool.wait_ge(sem("shifted"), 10)
            link(G.tensor_tensor(a_rk, a_z[:, 0:4, :], a_z[:, 4:8, :], ALU.mult))
            for t in range(4):
                ins = G.tensor_scalar(a_rk[:, t, :], a_rk[:, t, :], pc("rk", t), None, ALU.mult)
            ins.then_inc(sem("rk"), 1)
            pool.wait_ge(sem("ein"), 1)
            G.tensor_tensor(kr[:, :, 1, :], a_z[:, 0:4, :], a_ein, ALU.mult).then_inc(sem("rp"), 1)
            stage_read(pool, "za")
            G.tensor_copy(a_lc, a_zp[:, :, SEQ:ZPW:5]).then_inc(sem("last_rows"), 1)
            pool.wait_ge(sem("last_rows"), 1)
            pool.dma_start(a["shift_out"], a_lc).then_inc(sem("stored"), 16)
            pool.wait_ge(sem("a_used"), 1)
            pool.wait_ge(sem("exps"), 1)
            G.tensor_tensor(m(A_A, 1152), m(A_A, 1152), m(A_EE, 1152), ALU.mult).then_inc(sem("operands_pool"), 1)
            for j in range(2):
                for s in range(2):
                    pool.wait_ge(*out(("gram", j, s, 3)))
                invert_pool(pool, "a", j, AT, AM)
            for s in range(2):
                pool.wait_ge(*out(("Q1", 1, s)))
                pool.wait_ge(*out(("G", 1, s, 1)))
                pool.wait_ge(*out(("H", 1, s, 1)))
            pool.dma_start(a_s0, a["rwkv_in"]).then_inc(sem("rwkv_in"), 16)
            link(G.memset(a_kb, 0.0))
            for t in range(4):
                for b in range(DB):
                    ins = G.tensor_copy(a_kb[:, t, b * 68:b * 68 + 4], kr[:, t, 0, SEQ + 4 * b:SEQ + 4 * b + 4])
            ins.then_inc(sem("s_kb"), 1)
            for s in range(2):
                pool.wait_ge(*out(("sgram", s)))
            lt = s_at[:, :, 0:NS]
            G.tensor_tensor(s_a, lt, bc(C("lev1", NROW)[:, 0:NS], 1, 8), ALU.mult)
            link(G.tensor_tensor(s_tt, lt, bc(C("lev0", NROW)[:, 0:NS], 1, 8), ALU.mult))
            G.tensor_tensor(s_tt, bc(C("ident", NROW)[:, 0:NS], 1, 8), s_tt, ALU.subtract).then_inc(sem("s_masked"), 1)
            vn = a_nat[NROW, 2, 0, :].rearrange("p (h v) -> p h v", h=8)
            G.tensor_tensor(s_vb, bc(vn, 2, DB), bc(bc(C("selb", NROW), 1, 8), 3, 64),
                            ALU.mult).then_inc(sem("s_vb"), 1)
            pool.wait_ge(*out(("chain", 3, 0)))
            pool.wait_ge(*out(("chain", 3, 1)))
            pool.dma_start(a["rwkv_p"], a_s[:, 2, :, :]).then_inc(sem("stored"), 16)
            for t in range(4):
                pool.wait_ge(*out(("sS", t)))
            pool.dma_start(a["rwkv_s"], a_s0).then_inc(sem("stored"), 16)
            pool.wait_ge(*out(("gnv", 3)))
            pool.dma_start(b_s0, a["ret_in"]).then_inc(sem("ret_in"), 16)
            for t in range(8):
                pool.wait_ge(*full(("rot", t)))
                G.tensor_tensor(b_z[:, t, :], b_z[:, t, :], C("cos"), ALU.mult).then_inc(sem("cosine"), 1)
            pool.wait_ge(sem("gn_done"), 4)
            G.tensor_tensor(m(A_GATE, 1152), m(A_LD, 1152), m(A_GATE, 1152), ALU.mult).then_inc(sem("y_rwkv"), 1)
            pool.wait_ge(sem("stored"), 48)
            pool.wait_ge(*out(("rvn", 2)))
            for h in range(4):
                ins = G.tensor_tensor(b_vb[:, h, :, :], bc(b_vn[NROW, 2, h, :], 1, DB), bc(C("selb", NROW), 2, P),
                                      ALU.mult)
            ins.then_inc(sem("b_vb"), 1)
            pool.wait_ge(*out(("rS", 1)))
            pool.dma_start(a["ret_p"], b_s[:, 1, :, :]).then_inc(sem("stored"), 16)
            low_parts(pool, G, 2, 1, lambda d: a_gate[:, d, :] if d < 4 else b_ot[:, d - 4, :])
            for h in range(4):
                for q in range(2):
                    pool.wait_ge(*out(("rsS", h, q)))
            pool.dma_start(a["ret_s"], b_s0).then_inc(sem("stored"), 16)

        def invert_pool(pool, tag, j, at_, am):
            for l in range(1, LEVELS):
                for s in range(2):
                    if l > 1:
                        pool.wait_ge(*full(("Y", tag, j, s, l - 1)))
                    nc.gpsimd.tensor_tensor(am[s], at_[s][:, :, 0:P], mask4(f"lev{l}", P),
                                            ALU.mult).then_inc(sem("masked"), 1)

        g_c = m(G_C, QKV, T)
        g_zg = m(G_ZG, 8, T)
        g_l2 = [r[:], m(G_L2, 8 * T)]
        g_raw = m(G_RAW, QKV, PADW)
        g_acc = m(G_ACC, 2, CONVW)
        g_cin = m(G_CIN, QKV, DB, 3)
        g_cout = m(G_COUT, QKV, 27)
        g_sq = m(G_SQ, 4, T)
        g_xk = m(G_XK, 3, 4, 2 * P)
        g_kd = m(G_KD, 3, 4, P)
        g_gt, g_h = m(G_GT, 4, 4, P), m(G_H, 4, 4, P)
        g_s = m(G_S, 3, 4, P)
        g_s0 = [s0_space[:, 1024 * h:1024 * h + 1024].rearrange("p (b v) -> p b v", b=DB) for h in range(4)]
        g_lt, g_aq, g_tm, g_tt, g_ym, g_am = ([m(G_BATCH + 3072 * s + 512 * i, 4, P) for s in range(2)]
                                              for i in range(6))
        g_kb = r[:, 0:1152].rearrange("p (h t) -> p h t", h=4)
        g_q = r[:, 1152:2304].rearrange("p (h t) -> p h t", h=4)
        q_kq = m(G_BATCH, 4, 512)
        q_lt, q_aq, q_tm, q_tt, q_ym, q_am = (m(G_BATCH + 2304 + 128 * i, 4, NS, rows=NROW) for i in range(6))
        q_dx, q_dy = (m(G_BATCH + 3072 + 128 * i, 4, NS, rows=NROW) for i in range(2))
        q_x, q_u = (m(G_BATCH + 3328 + 512 * i, 4, P, rows=NROW) for i in range(2))
        q_tmp = m(G_BATCH + 4352, 4, NS)
        QROW = slice(32, 64)
        q_o = m(G_BATCH + 4480, 4, P, rows=QROW)
        q_ub = m(G_XK, 2, DB, P, rows=NROW)
        g_tmp = m(G_BATCH + 6144, 4, NS)
        _o = CONST_GD.shape[1]
        rows_b = mixc[0:HC, _o:_o + T]
        R32 = slice(32, 32 + HC)
        rows_g = mixc[R32, _o + T:_o + 2 * T]
        rows_e = mixc[R32, _o + 2 * T:_o + 3 * T]
        g_tok = mixc[:, _o + 864:_o + 864 + 96].rearrange("p (j c) -> p j c", j=3)
        g_egc = mixc[:, _o + 960:_o + 960 + 48].rearrange("p (h c) -> p h c", h=4)
        g_gb = mixc[:, _o + 1008:_o + 1008 + 1152].rearrange("p (h t) -> p h t", h=4)

        def gmask(s, j, l):
            return (s * (LEVELS - 1) + l - 1) * 2 + j + 1

        def gdn_tensor(pe, env):
            start, stage = env["start"], env["stage"]

            def fin(ins, key):
                ins.then_inc(filled[bank_of(key)], 1)

            stage("ba", 5)
            stage("qk", 5)
            pe.wait_ge(sem("const_gd_in"), 16)
            pe.wait_ge(sem("rows"), 2)
            bank = start(("gtokb", 0))
            for j in range(3):
                w = P if j < 2 else NS
                mm = pe.transpose(bank[0:w, 8 * j:8 * j + 8], rows_b[:, tok(j)], C("ident")[0:8, 0:8])
            fin(mm, ("gtokb", 0))
            bank = start(("gtok", 0))
            for j in range(3):
                w = P if j < 2 else NS
                pe.transpose(bank[0:w, 16 * j:16 * j + 8], rows_g[:, tok(j)], C("ident")[R32, 32:40])
                mm = pe.transpose(bank[0:w, 16 * j + 8:16 * j + 16], rows_e[:, tok(j)], C("ident")[R32, 32:40])
            fin(mm, ("gtok", 0))
            def l2_sums(k):
                for t in (2 * k - 2, 2 * k - 1):
                    if t < 0:
                        continue
                    pe.wait_ge(sem("qk_sq"), t + 1)
                    bank = start(("dl2", t))
                    fin(pe.matmul(bank[:, 0:T], C("ones"), g_sq[:, t % 4, :], start=True, stop=True), ("dl2", t))

            stage("v", 5, l2_sums)
            l2_sums(8)
            J2 = slice(SEQ, T)
            sel = C("sel8").rearrange("p (h c) -> p h c", h=8)

            def on_all_rows(name, s):
                src, rows = (rows_b, slice(0, 8)) if name == "dbb" else (rows_g, R32)
                for h in range(4):
                    key = (name, s, h)
                    bank = start(key)
                    fin(pe.matmul(bank[:, 0:T], sel[rows, 4 * s + h, :], src, start=True, stop=True), key)

            def square_sums(t0):
                for t in range(t0, t0 + 4):
                    pe.wait_ge(sem("o_sq"), t + 1)
                    bank = start(("dnrm", t))
                    fin(pe.matmul(bank[:, 0:T], C("ones"), g_c[:, t, :], start=True, stop=True), ("dnrm", t))

            on_all_rows("dgb", 0)
            stage("zg", 5)
            on_all_rows("dbb", 0)
            for s in range(2):
                pe.wait_ge(sem("qk_norm"), 1)
                pe.wait_ge(*out(("dbb", s, 3)))
                for j in range(2):
                    for q in range(3):
                        key = ("dgram", s, j, q)
                        bank = start(key)
                        for h in range(4):
                            k_, kb_, q_ = (g_c[:, 8 + 4 * s + h, tok(j)], g_kb[:, h, tok(j)],
                                           g_c[:, 4 * s + h, tok(j)])
                            lhs, rhs = ((k_, kb_), (k_, q_), (kb_, k_))[q]
                            mm = pe.matmul(bank[:, h * P:(h + 1) * P], lhs, rhs, start=True, stop=True)
                        fin(mm, key)
                for l in range(1, LEVELS):
                    for j in range(2):
                        key = ("dY", s, j, l)
                        bank = start(key)
                        pe.wait_ge(sem("g_masked"), gmask(s, j, l))
                        if l == 1:
                            pe.wait_ge(sem("g_t0"), 2 * s + j + 1)
                        else:
                            pe.wait_ge(*out(("dX", s, j, l - 1)))
                        for h in range(4):
                            mm = pe.matmul(bank[:, h * P:(h + 1) * P], g_am[j][:, h, :], g_tm[j][:, h, :],
                                           start=True, stop=True)
                        fin(mm, key)
                    if l < 4:
                        w = P if l < 3 else NS
                        for name, t0 in (("dvn", 16), ("dkn", 8)):
                            key = (name, s, l - 1)
                            bank = start(key)
                            for h in range(4):
                                mm = pe.transpose(bank[0:w, h * P:(h + 1) * P],
                                                  g_c[:, t0 + 4 * s + h, tok(l - 1)], C("ident"))
                            fin(mm, key)
                    for j in range(2):
                        if l == 1:
                            pe.wait_ge(sem("g_tt0"), 2 * s + j + 1)
                        else:
                            pe.wait_ge(*out(("dXT", s, j, l - 1)))
                        pe.wait_ge(*out(("dY", s, j, l)))
                        for name in ("dX", "dXT")[(0 if l < LEVELS - 1 else 1):]:
                            key = (name, s, j, l)
                            bank = start(key)
                            lhs, rhs = (g_tt[j], g_ym[j]) if name == "dX" else (g_ym[j], g_tt[j])
                            for h in range(4):
                                mm = pe.matmul(bank[:, h * P:(h + 1) * P], lhs[:, h, :], rhs[:, h, :],
                                               start=True, stop=True)
                            fin(mm, key)
                for j in range(2):
                    pe.wait_ge(*out(("dXT", s, j, LEVELS - 1)))
                    pe.wait_ge(*out(("dkn", s, j)))
                    pe.wait_ge(*out(("dvn", s, j)))
                    for q in range(2):
                        key = ("dUW", s, j, q)
                        bank = start(key)
                        for h in (2 * q, 2 * q + 1):
                            mm = pe.matmul(bank[:, (h % 2) * 256:(h % 2) * 256 + 256], g_tt[j][:, h, :],
                                           g_xk[:, j, h, :], start=True, stop=True)
                        fin(mm, key)
                    pe.wait_ge(*out(("dUW", s, j, 0)))
                    pe.wait_ge(*out(("dUW", s, j, 1)))
                    pe.wait_ge(*out(("dgram", s, j, 1)))
                    for name, c0 in (("dO0", 0), ("dQ1", P)):
                        bank = start((name, s, j))
                        for h in range(4):
                            mm = pe.matmul(bank[:, h * P:(h + 1) * P], g_xk[:, j, h, c0:c0 + P], g_aq[j][:, h, :],
                                           start=True, stop=True)
                        fin(mm, (name, s, j))
                    for name in ("dG", "dH"):
                        for c in range(2):
                            rows = slice(64 * c, 64 * c + 64)
                            bank = start((name, s, j, c))
                            for h in range(4):
                                u_, w_, kd_ = g_xk[rows, j, h, 0:P], g_xk[rows, j, h, P:2 * P], g_kd[rows, j, h, :]
                                lhs, rhs = (w_, kd_) if name == "dG" else (kd_, u_)
                                mm = pe.matmul(bank[:, h * P:(h + 1) * P], lhs, rhs, start=True, stop=True)
                            fin(mm, (name, s, j, c))

                def state(c, h):
                    return g_h[:, 0, h, :] if c == 1 else g_s[:, c - 2, h, :]

                pe.wait_ge(*out(("dG", s, 1, 1)))
                pe.wait_ge(*out(("dH", s, 1, 1)))
                for c in range(1, 4):
                    if c > 1:
                        pe.wait_ge(*out(("dchain", s, c - 1)))
                    bank = start(("dchain", s, c))
                    for h in range(4):
                        mm = pe.matmul(bank[:, h * P:(h + 1) * P], g_gt[:, c, h, :], state(c, h),
                                       start=True, stop=True)
                    fin(mm, ("dchain", s, c))
                pe.wait_ge(*out(("dQ1", s, 1)))
                for h in range(4):
                    bank = start(("dOS", s, h))
                    for c in range(1, 4):
                        mm = pe.matmul(bank[:, c * 64:(c + 1) * 64], state(c, h), g_q[:, h, c * 64:(c + 1) * 64],
                                       start=True, stop=True)
                    fin(mm, ("dOS", s, h))
                if s == 0:
                    on_all_rows("dgb", 1)
                pe.wait_ge(sem("q_kb"), s + 1)
                pe.wait_ge(sem("gdn_in"), 64 * (s + 1))
                bank = start(("dsX", s))
                for h in range(4):
                    for b in range(DB):
                        mm = pe.matmul(bank[0:64, h * P:(h + 1) * P], q_kq[:, h, 64 * b:64 * b + 64],
                                       g_s0[h][:, b, :], start=(b == 0), stop=(b == DB - 1))
                fin(mm, ("dsX", s))
                for q in range(3):
                    key = ("dsgram", s, q)
                    bank = start(key)
                    for h in range(4):
                        k_, kb_, q_ = g_c[:, 8 + 4 * s + h, J2], g_kb[:, h, J2], g_c[:, 4 * s + h, J2]
                        lhs, rhs = ((k_, kb_), (k_, q_), (kb_, k_))[q]
                        mm = pe.matmul(bank[NROW, h * NS:(h + 1) * NS], lhs, rhs, start=True, stop=True)
                    fin(mm, key)
                pe.wait_ge(sem("q_masked"), s + 1)
                pe.wait_ge(sem("q_t0"), s + 1)
                bank = start(("dsY", s))
                for h in range(4):
                    mm = pe.matmul(bank[NROW, h * NS:(h + 1) * NS], q_am[:, h, :], q_tm[:, h, :],
                                   start=True, stop=True)
                fin(mm, ("dsY", s))
                pe.wait_ge(*out(("dsY", s)))
                bank = start(("dsXT", s))
                for h in range(4):
                    mm = pe.matmul(bank[NROW, h * NS:(h + 1) * NS], q_ym[:, h, :], q_tt[:, h, :],
                                   start=True, stop=True)
                fin(mm, ("dsXT", s))
                pe.wait_ge(*out(("dsXT", s)))
                pe.wait_ge(*out(("dsX", s)))
                bank = start(("dsU", s))
                for h in range(4):
                    mm = pe.matmul(bank[NROW, h * P:(h + 1) * P], q_tt[:, h, :], q_x[:, h, :],
                                   start=True, stop=True)
                fin(mm, ("dsU", s))
                pe.wait_ge(*out(("dsU", s)))
                bank = start(("dsO", s))
                for h in range(4):
                    mm = pe.matmul(bank[QROW, h * P:(h + 1) * P], q_aq[:, h, :], q_u[:, h, :], start=True, stop=True)
                fin(mm, ("dsO", s))
                pe.wait_ge(*out(("dsO", s)))
                bank = start(("dsT", s))
                for h in range(4):
                    mm = pe.transpose(bank[:, h * NS:(h + 1) * NS], q_o[:, h, :], C("ident")[QROW, 32:64])
                fin(mm, ("dsT", s))
                if s == 0:
                    on_all_rows("dbb", 1)
                    square_sums(0)
                for h in range(4):
                    if s == 1 and h == 1:
                        square_sums(4)
                    pe.wait_ge(sem("q_ub"), 4 * s + h + 1)
                    for q in range(2):
                        bank = start(("dsS", s, h, q))
                        fin(pe.matmul(bank[:, 0:512], g_kd[NROW, 2, h, :], q_ub[:, h % 2, 4 * q:4 * q + 4, :],
                                      start=True, stop=True), ("dsS", s, h, q))
            stage("gdo", 6)

        def gdn_scalar(act, env):
            link = env["link"]

            def jb(key, w=512):
                return jobb[bank_of(key)][:, 0:w]

            def copy(key, dst, src, scale=1.0):
                nc.scalar.activation(dst, src, ACT.Copy, scale=scale).then_inc(drained[bank_of(key)], 1)

            def beta(i, j, u0, use):
                act.wait_ge(unit_done, u0 + 1)
                act.wait_ge(sem("const_gd_in"), 16)
                nc.scalar.activation(rows_b, gemm[0][0:HC, 0:T], ACT.Sigmoid)
                nc.scalar.activation(rows_g, gemm[0][R32, 0:T], ACT.Identity, bias=pc("dtb", 0, R32)
                                     ).then_inc(bank_free[0], 1)

            def conv_out(k, slot):
                act.wait_ge(sem("conv"), k * 4 + 4)
                nc.scalar.activation(g_c[:, k, 0:SEQ], g_acc[:, slot, 0:SEQ], ACT.Silu)
                nc.scalar.activation(g_c[:, k, SEQ:T].rearrange("p (b s) -> p b s", s=DS), acc_sample(slot),
                                     ACT.Silu).then_inc(sem("conv_out"), 1)

            def conv_in(k0, behind):
                def consume(i, j, u0, use):
                    k = i * 4 + (k0 + j)
                    act.wait_ge(unit_done, i * 4 + (u0 + j + 1))
                    nc.scalar.activation(g_raw[:, k, 3:3 + SEQ], gemm[j][:, 0:SEQ], ACT.Copy)
                    nc.scalar.activation(g_raw[:, k, 3 + SEQ:PADW].rearrange("p (b s) -> p b s", s=7)[:, :, 3:7],
                                         gemm[j][:, SEQ:T].rearrange("p (b s) -> p b s", s=DS), ACT.Copy
                                         ).then_inc(bank_free[j], 1)
                    if k0 or not isinstance(i, int) or i or j:
                        conv_out(i * 4 + (k0 + j - 1), (j - 1) % 2)
                    if behind:
                        behind(4 * i + j)
                return consume

            def squares(k):
                for t in (2 * k, 2 * k + 1):
                    act.wait_ge(sem("conv_out"), t + 1)
                    if t >= 4:
                        act.wait_ge(*full(("dl2", t - 4)))
                    nc.scalar.activation(g_sq[:, t % 4, :], g_c[:, t, :], ACT.Square).then_inc(sem("qk_sq"), 1)

            def gate(i, j, u0, use):
                k = 4 * i + j
                act.wait_ge(unit_done, u0 + k + 1)
                nc.scalar.activation(g_zg[:, k, :], gemm[j][:, 0:T], ACT.Copy).then_inc(bank_free[j], 1)
                if k == 0:
                    for h in range(4):
                        key = ("dgb", 0, h)
                        act.wait_ge(*full(key))
                        copy(key, g_gb[:, h, :], jb(key, T))
                elif k in (1, 2):
                    act.wait_ge(*out(("dl2", 8 * k - 1)))
                    nc.scalar.activation(g_l2[k - 1], g_l2[k - 1], ACT.Ln).then_inc(sem("qk_ln"), 1)
                elif k in (3, 4):
                    act.wait_ge(sem("qk_ln"), k - 2)
                    nc.scalar.activation(g_l2[k - 3], g_l2[k - 3], ACT.Exp, scale=-0.5).then_inc(sem("qk_root"), 1)
                elif k == 5:
                    decays(0)

            def decays(s):
                act.wait_ge(sem("g_dx"), 2 * s + 2)
                act.wait_ge(sem("g_dy"), 2 * s + 2)
                act.wait_ge(sem("q_dx"), s + 1)
                for j in range(2):
                    nc.scalar.activation(g_ym[j], g_ym[j], ACT.Exp)
                    nc.scalar.activation(g_am[j], g_am[j], ACT.Exp, scale=-1.0).then_inc(sem("g_dexp"), 1)
                nc.scalar.activation(g_gb, g_gb, ACT.Exp).then_inc(sem("g_eg"), 1)

            env["stage"]("ba", beta)
            stage_read(act, "ba")
            link(nc.scalar.activation(rows_e, rows_g, ACT.Abs))
            link(nc.scalar.activation(rows_e, rows_e, ACT.Exp, scale=-1.0))
            nc.scalar.activation(par[R32, PCOLS["alog"][0]:PCOLS["alog"][0] + 1], pc("alog", 0, R32), ACT.Exp)
            nc.scalar.activation(rows_e, rows_e, ACT.Ln, bias=C("eps", R32)[:, 5:6]).then_inc(sem("soft"), 1)
            env["stage"]("qk", conv_in(0, None))
            env["stage"]("v", conv_in(16, squares))
            conv_out(QKV - 1, (QKV - 1) % 2)
            act.wait_ge(*out(("gtok", 0)))
            link(nc.scalar.activation(g_tok[:, 0:2, 24:32], g_tok[:, 0:2, 8:16], ACT.Exp))
            link(nc.scalar.activation(g_tok[NROW, 2, 24:32], g_tok[NROW, 2, 8:16], ACT.Exp))
            nc.scalar.activation(g_tok[:, 0:2, 16:24], g_tok[:, 0:2, 16:24], ACT.Exp)
            nc.scalar.activation(g_tok[NROW, 2, 16:24], g_tok[NROW, 2, 16:24], ACT.Exp).then_inc(sem("tok_exp"), 1)
            env["stage"]("zg", gate)
            for s in range(2):
                for l in range(1, LEVELS):
                    for j in range(2):
                        key = ("dY", s, j, l)
                        act.wait_ge(*full(key))
                        copy(key, g_ym[j], jb(key).rearrange("p (h t) -> p h t", h=4))
                    if l < 4:
                        w = slice(0, P if l < 3 else NS)
                        key = ("dvn", s, l - 1)
                        act.wait_ge(*full(key))
                        for h in range(4):
                            ins = nc.scalar.activation(g_xk[w, l - 1, h, 0:P], jb(key)[w, h * P:(h + 1) * P], ACT.Copy,
                                                       scale=g_tok[w, l - 1, 4 * s + h:4 * s + h + 1])
                        ins.then_inc(drained[bank_of(key)], 1)
                for j in range(2):
                    for q in range(2):
                        key = ("dUW", s, j, q)
                        act.wait_ge(*full(key))
                        src = jb(key).rearrange("p (h x) -> p h x", h=2)
                        nc.scalar.activation(g_xk[:, j, 2 * q:2 * q + 2, 0:P], src[:, :, 0:P], ACT.Copy)
                        copy(key, g_xk[:, j, 2 * q:2 * q + 2, P:2 * P], src[:, :, P:2 * P], -1.0)
                    key = ("dO0", s, j)
                    act.wait_ge(*full(key))
                    copy(key, g_c[:, 16 + 4 * s:20 + 4 * s, tok(j)], jb(key).rearrange("p (h t) -> p h t", h=4))
                    for c in range(2):
                        key = ("dH", s, j, c)
                        act.wait_ge(*full(key))
                        copy(key, g_h[:, 2 * j + c, :, :], jb(key).rearrange("p (h t) -> p h t", h=4))
                act.wait_ge(sem("q_dmin"), s + 1)
                nc.scalar.activation(q_dx, q_dx, ACT.Exp)
                nc.scalar.activation(q_dy, q_dy, ACT.Exp, scale=-1.0).then_inc(sem("q_dexp"), 1)
                if s == 0:
                    act.wait_ge(sem("q_ke"), 1)
                    for h in range(4):
                        key = ("dgb", 1, h)
                        act.wait_ge(*full(key))
                        copy(key, g_gb[:, h, :], jb(key, T))
                key = ("dsX", s)
                act.wait_ge(*full(key))
                nc.scalar.activation(q_o, jb(key)[QROW].rearrange("p (h v) -> p h v", h=4), ACT.Copy
                                     ).then_inc(sem("q_os"), 1)
                key = ("dsY", s)
                act.wait_ge(*full(key))
                copy(key, q_ym, jb(key, P)[NROW].rearrange("p (h t) -> p h t", h=4))
                key = ("dsU", s)
                act.wait_ge(*full(key))
                copy(key, q_u, jb(key)[NROW].rearrange("p (h v) -> p h v", h=4))
                key = ("dsT", s)
                act.wait_ge(*full(key))
                copy(key, g_c[:, 16 + 4 * s:20 + 4 * s, SEQ:T], jb(key, P).rearrange("p (h t) -> p h t", h=4))
                act.wait_ge(*out(("dOS", s, 3)))
                act.wait_ge(*out(("dsT", s)))
                for t in range(4 * s, 4 * s + 4):
                    nc.scalar.activation(g_c[:, t, :], g_c[:, 16 + t, :], ACT.Square).then_inc(sem("o_sq"), 1)
                if s == 0:
                    nc.scalar.activation(g_zg, g_zg, ACT.Silu).then_inc(sem("gated"), 1)
                for t in range(4 * s, 4 * s + 4):
                    key = ("dnrm", t)
                    act.wait_ge(*full(key))
                    nc.scalar.activation(g_c[:, 8 + t, :], jb(key, T), ACT.Ln, bias=C("eps")[:, 4:5], scale=1.0 / P
                                         ).then_inc(drained[bank_of(key)], 1)
                act.wait_ge(*out(key))
                half = m(G_C + (8 + 4 * s) * T, 4 * T)
                nc.scalar.activation(half, half, ACT.Exp, scale=-0.5).then_inc(sem("rms"), 1)
                if s == 0:
                    decays(1)
            act.wait_ge(sem("y_gdn"), 2)
            act.wait_ge(sem("gdn_s_stored"), 128)
            for d in range(DT):
                nc.scalar.activation(xhi[:, d, :], g_c[:, 16 + d, :], ACT.Copy).then_inc(x_hi, 1)
            env["stage"]("gdo", env["idle"])

        def acc_sample(slot):
            at = G_ACC + CONVW * slot + SEQ + 3
            return M[:, at:at + 53 + 3].rearrange("p (b s) -> p b s", s=7)[:, :, 0:DS]

        def gdn_vector(dve, env):
            link = env["link"]
            V = nc.vector

            def jb(key, w=512):
                return jobb[bank_of(key)][:, 0:w]

            def read(ins, key):
                ins.then_inc(drained[bank_of(key)], 1)

            def none(i, j, u0, use):
                pass

            def conv(k0, behind):
                def consume(i, j, u0, use):
                    k = i * 4 + (k0 + j)
                    dve.wait_ge(bank_free[j], i + (use[j] + 1))
                    wait_count(dve, sem("conv_out"), i * 4 + (k0 + j - 1))
                    for q in range(4):
                        cw = conv_col(q, k)
                        src = g_raw[:, k, q:q + CONVW]
                        if q == 0:
                            ins = V.tensor_scalar(g_acc[:, j % 2, :], src, cw, None, ALU.mult)
                        else:
                            dve.wait_ge(sem("conv"), k * 4 + q)
                            ins = V.scalar_tensor_tensor(out=g_acc[:, j % 2, :], in0=src, scalar=cw,
                                                         in1=g_acc[:, j % 2, :], op0=ALU.mult, op1=ALU.add)
                        ins.then_inc(sem("conv"), 1)
                    if behind:
                        behind(4 * i + j)
                return consume

            def l2_max(k):
                for t in (2 * k - 4, 2 * k - 3):
                    if t >= 0:
                        key = ("dl2", t)
                        dve.wait_ge(*full(key))
                        dst = g_l2[t // 8][:, (t % 8) * T:(t % 8 + 1) * T]
                        read(V.tensor_scalar(dst, jb(key, T), 1e-12, None, ALU.max), key)

            def conv_col(q, k):
                at = PCOLS["conv"][0] + QKV * q
                return par[:, at:at + QKV].rearrange("p (k o) -> p k o", o=1)[:, k, :]

            env["stage"]("ba", none)
            dve.wait_ge(sem("conv_pad"), 1)
            dve.wait_ge(sem("soft"), 1)
            link(V.tensor_scalar(rows_g, rows_g, 0.0, None, ALU.max))
            link(V.tensor_tensor(rows_g, rows_g, rows_e, ALU.add))
            link(V.tensor_scalar(rows_g, rows_g, pc("alog", 0, R32), -1.0, ALU.mult, ALU.mult))
            link(V.tensor_tensor_scan(out=rows_e, data0=C("scan", R32), data1=rows_g, initial=0.0,
                                      op0=ALU.mult, op1=ALU.add))
            link(V.tensor_copy(rows_g, rows_e))
            for lo, hi, n in ((0, SEQ, CH), (SEQ, T, DS)):
                a_ = rows_g[:, lo:hi].rearrange("p (c s) -> p c s", s=n)
                o_ = rows_e[:, lo:hi].rearrange("p (c s) -> p c s", s=n)
                V.tensor_tensor(o_, a_[:, :, n - 1:n].to_broadcast([HC, (hi - lo) // n, n]), a_,
                                ALU.subtract).then_inc(sem("rows"), 1)
            env["stage"]("qk", conv(0, None))
            for key, c0, n in ((("gtokb", 0), 0, 8), (("gtok", 0), 8, 16)):
                dve.wait_ge(*full(key))
                V.tensor_copy(g_tok[:, 0:2, c0:c0 + n], jb(key, 2 * n).rearrange("p (j c) -> p j c", j=2))
                read(V.tensor_copy(g_tok[NROW, 2, c0:c0 + n], jb(key, 3 * n)[NROW, 2 * n:3 * n]), key)
            env["stage"]("v", conv(16, l2_max))
            l2_max(8)
            l2_max(9)
            V.tensor_copy(g_cout[:, :, 0:3], g_raw[:, :, SEQ:SEQ + 3])
            V.tensor_copy(g_cout[:, :, 3:27].rearrange("p k (b s) -> p k b s", s=3),
                          g_raw[:, :, 3 + SEQ:PADW].rearrange("p k (b s) -> p k b s", s=7)[:, :, :, 4:7]
                          ).then_inc(sem("conv_rows"), 1)

            def between(i, j, u0, use):
                k = 4 * i + j
                if k == 1:
                    differences(0)
                elif k == 5:
                    dve.wait_ge(sem("qk_root"), 1)
                    V.scalar_tensor_tensor(out=m(G_C, 8 * T), in0=m(G_C, 8 * T), scalar=QSCALE, in1=g_l2[0],
                                           op0=ALU.mult, op1=ALU.mult)
                elif k == 6:
                    dve.wait_ge(sem("qk_root"), 2)
                    V.tensor_tensor(m(G_C + 8 * T, 8 * T), m(G_C + 8 * T, 8 * T), g_l2[1],
                                    ALU.mult).then_inc(sem("qk_norm"), 1)

            def differences(s):
                for h in range(4):
                    dve.wait_ge(*out(("dgb", s, h)))
                for j in range(2):
                    for h in range(4):
                        gcn = g_tok[:, j, 8 + 4 * s + h:9 + 4 * s + h]
                        ins = V.tensor_scalar(g_ym[j][:, h, :], g_gb[:, h, tok(j)], gcn, 0.0, ALU.subtract, ALU.min)
                    ins.then_inc(sem("g_dx"), 1)
                V.tensor_copy(g_tmp, g_gb[:, :, SEQ:T]).then_inc(sem("q_dx"), 1)

            dve.wait_ge(sem("tok_exp"), 1)
            for rows, j in ((slice(0, P), slice(0, 2)), (NROW, slice(2, 3))):
                link(V.tensor_tensor(g_tok[rows, j, 24:32], g_tok[rows, j, 24:32], g_tok[rows, j, 0:8], ALU.mult))
            env["stage"]("zg", between)
            dve.wait_ge(sem("qk_norm"), 1)

            def beta_k(s):
                for h in range(4):
                    key = ("dbb", s, h)
                    dve.wait_ge(*full(key))
                    read(V.tensor_tensor(g_kb[:, h, :], g_c[:, 8 + 4 * s + h, :], jb(key, T), ALU.mult), key)

            def gated_norm(s):
                dve.wait_ge(sem("rms"), s + 1)
                o = m(G_C + (16 + 4 * s) * T, 4 * T)
                link(V.tensor_tensor(o, o, m(G_C + (8 + 4 * s) * T, 4 * T), ALU.mult))
                dve.wait_ge(sem("gated"), 1)
                V.scalar_tensor_tensor(out=o, in0=o, scalar=pc("ng"), in1=m(G_ZG + 4 * s * T, 4 * T), op0=ALU.mult,
                                       op1=ALU.mult).then_inc(sem("y_gdn"), 1)

            beta_k(0)
            for s in range(2):
                hs = slice(4 * s, 4 * s + 4)
                up = bc(C("up64")[:, P:2 * P], 1, 4)
                for j in range(2):
                    dve.wait_ge(sem("g_dexp"), 2 * s + j + 1)
                    link(V.tensor_tensor(g_ym[j], g_ym[j], up, ALU.mult))
                    for q, (dst, dec) in enumerate(((g_lt, g_ym), (g_aq, g_ym), (g_tm, g_am))):
                        key = ("dgram", s, j, q)
                        dve.wait_ge(*full(key))
                        if q == 2:
                            dve.wait_ge(sem("g_dmask"), 2 * s + j + 1)
                        read(V.tensor_tensor(dst[j], jb(key).rearrange("p (h t) -> p h t", h=4), dec[j],
                                             ALU.mult), key)
                    dve.wait_ge(*out(key))
                    V.tensor_tensor(g_tm[j], mask4("ident", P), g_tm[j], ALU.subtract).then_inc(sem("g_t0"), 1)
                for j in range(2):
                    link(V.tensor_tensor(g_tt[j], g_lt[j], mask4("lev0", P), ALU.mult))
                    V.tensor_tensor(g_tt[j], mask4("ident", P), g_tt[j], ALU.subtract).then_inc(sem("g_tt0"), 1)
                dve.wait_ge(sem("g_eg"), s + 1)
                V.tensor_tensor(g_q, g_c[:, hs, :], g_gb, ALU.mult)
                V.tensor_copy(g_egc[:, :, 0:4], g_gb[:, :, CH - 1:SEQ:CH])
                link(V.tensor_copy(g_egc[:, :, 4:12], g_gb[:, :, SEQ + DS - 1:T:DS]))
                for l in range(1, LEVELS):
                    if l < 4:
                        j = l - 1
                        w = slice(0, P if j < 2 else NS)
                        key = ("dkn", s, j)
                        dve.wait_ge(*full(key))
                        src = jb(key)[w].rearrange("p (h c) -> p h c", h=4)
                        V.tensor_tensor(g_xk[w, j, :, P:2 * P], src, bc(g_tok[w, j, 24 + 4 * s:28 + 4 * s], 2, P),
                                        ALU.mult)
                        read(V.tensor_tensor(g_kd[w, j, :, :], src, bc(g_tok[w, j, 16 + 4 * s:20 + 4 * s], 2, P),
                                             ALU.mult), key)
                    for j in range(2):
                        for name, dst in (("dX", g_tm), ("dXT", g_tt))[(0 if l < LEVELS - 1 else 1):]:
                            key = (name, s, j, l)
                            dve.wait_ge(*full(key))
                            read(V.tensor_tensor(dst[j], dst[j], jb(key).rearrange("p (h t) -> p h t", h=4),
                                                 ALU.subtract), key)
                for j in range(2):
                    key = ("dQ1", s, j)
                    dve.wait_ge(*full(key))
                    o = g_q[:, :, tok(j)]
                    read(V.tensor_tensor(o, jb(key).rearrange("p (h t) -> p h t", h=4), o, ALU.add), key)
                    for c in range(2):
                        key = ("dG", s, j, c)
                        dve.wait_ge(*full(key))
                        for h in range(4):
                            ck = 2 * j + c
                            ins = V.scalar_tensor_tensor(out=g_gt[:, ck, h, :], in0=C("ident"),
                                                         scalar=g_egc[:, h, ck:ck + 1],
                                                         in1=jobb[bank_of(key)][:, h * P:(h + 1) * P],
                                                         op0=ALU.mult, op1=ALU.add)
                        read(ins, key)
                for h in range(4):
                    gcn = g_tok[NROW, 2, 8 + 4 * s + h:9 + 4 * s + h]
                    V.tensor_scalar(q_dx[:, h, :], g_tmp[NROW, h, :], gcn, 0.0, ALU.subtract, ALU.min)
                    ins = V.tensor_scalar(q_dy[:, h, :], g_tmp[NROW, h, :], gcn, 0.0, ALU.subtract, ALU.max)
                ins.then_inc(sem("q_dmin"), 1)
                V.tensor_tensor(q_tmp, g_kb[:, :, SEQ:T], g_gb[:, :, SEQ:T], ALU.mult).then_inc(sem("q_ke"), 1)
                for j in range(2):
                    for c in range(2):
                        dve.wait_ge(*out(("dH", s, j, c)))
                for c in range(1, 4):
                    key = ("dchain", s, c)
                    dve.wait_ge(*full(key))
                    if s == 0:
                        dve.wait_ge(sem("conv_stored"), 16)
                    else:
                        dve.wait_ge(sem("gdn_p_stored"), 16)
                    read(V.tensor_tensor(g_s[:, c - 1, :, :], jb(key).rearrange("p (h v) -> p h v", h=4),
                                         g_h[:, c, :, :], ALU.add), key)
                dve.wait_ge(*out(("dO0", s, 1)))
                for h in range(4):
                    key = ("dOS", s, h)
                    dve.wait_ge(*full(key))
                    o = g_c[:, 16 + 4 * s + h, CH:SEQ]
                    read(V.tensor_tensor(o, jb(key, SEQ)[:, CH:SEQ], o, ALU.add), key)
                key = ("dsX", s)
                dve.wait_ge(*full(key))
                dve.wait_ge(sem("q_os"), s + 1)
                read(V.scalar_tensor_tensor(out=q_x, in0=jb(key)[NROW].rearrange("p (h v) -> p h v", h=4), scalar=-1.0,
                                            in1=g_xk[NROW, 2, :, 0:P], op0=ALU.mult, op1=ALU.add), key)
                dve.wait_ge(sem("q_dmask"), s + 1)
                for q, (dst, dec) in enumerate(((q_lt, q_dx), (q_aq, q_dx), (q_tm, q_dy))):
                    key = ("dsgram", s, q)
                    dve.wait_ge(*full(key))
                    read(V.tensor_tensor(dst, jb(key, P)[NROW].rearrange("p (h t) -> p h t", h=4), dec,
                                         ALU.mult), key)
                dve.wait_ge(*out(key))
                V.tensor_tensor(q_tm, bc(C("ident", NROW)[:, 0:NS], 1, 4), q_tm, ALU.subtract).then_inc(sem("q_t0"), 1)
                key = ("dsXT", s)
                dve.wait_ge(*full(key))
                dve.wait_ge(sem("q_masked"), s + 1)
                read(V.tensor_tensor(q_tt, q_tt, jb(key, P)[NROW].rearrange("p (h t) -> p h t", h=4),
                                     ALU.subtract), key)
                dve.wait_ge(*out(("dsU", s)))

                def by_sequence(h):
                    if h >= 2:
                        dve.wait_ge(*full(("dsS", s, h - 2, 1)))
                    V.tensor_tensor(q_ub[:, h % 2, :, :], bc(q_u[:, h, :], 1, DB), bc(C("selb", NROW), 2, P),
                                    ALU.mult).then_inc(sem("q_ub"), 1)

                key = ("dsO", s)
                dve.wait_ge(*full(key))
                read(V.tensor_tensor(q_o, jb(key)[QROW].rearrange("p (h v) -> p h v", h=4), q_o, ALU.add), key)
                by_sequence(0)
                by_sequence(1)
                if s == 0:
                    differences(1)
                    beta_k(1)
                for h in range(4):
                    dve.wait_ge(sem("s0_scaled"), 4 * s + h + 1)
                    for q in range(2):
                        key = ("dsS", s, h, q)
                        dve.wait_ge(*full(key))
                        o = g_s0[h][:, 4 * q:4 * q + 4, :]
                        read(V.tensor_tensor(o, o, jb(key).rearrange("p (b v) -> p b v", b=4), ALU.add), key)
                    if h < 2:
                        by_sequence(h + 2)
                gated_norm(s)
            dve.wait_ge(sem("gdn_s_stored"), 128)
            low_parts(dve, V, 6, 0, lambda d: g_c[:, 16 + d, :])
            env["stage"]("gdo", env["residual"](ALPHA, "out"))

        def gdn_pool(pool, env):
            link = env["link"]
            G = nc.gpsimd
            stage_read(pool, "down2")
            pool.dma_start(g_cin, a["conv_in"]).then_inc(sem("conv_in"), 16)
            G.memset(g_raw[:, :, 0:3], 0.0)
            pool.wait_ge(sem("conv_in"), 16)
            G.tensor_copy(g_raw[:, :, 3 + SEQ:PADW].rearrange("p k (b s) -> p k b s", s=7)[:, :, :, 0:3],
                          g_cin).then_inc(sem("conv_pad"), 1)
            pool.wait_ge(sem("conv_rows"), 1)
            pool.dma_start(a["conv_out"], g_cout).then_inc(sem("conv_stored"), 16)

            def states_in(s):
                for h in range(4):
                    pool.dma_start(g_s0[h], a["gdn_in"][:, 4 * s + h]).then_inc(sem("gdn_in"), 16)

            def differences(s):
                for h in range(4):
                    pool.wait_ge(*out(("dgb", s, h)))
                for j in range(2):
                    for h in range(4):
                        gcn = g_tok[:, j, 8 + 4 * s + h:9 + 4 * s + h]
                        ins = G.tensor_scalar(g_am[j][:, h, :], g_gb[:, h, tok(j)], gcn, 0.0, ALU.subtract, ALU.max)
                    ins.then_inc(sem("g_dy"), 1)

            def mask_decays(s):
                for j in range(2):
                    pool.wait_ge(sem("g_dexp"), 2 * s + j + 1)
                    G.tensor_tensor(g_am[j], g_am[j], mask4("low0", P), ALU.mult).then_inc(sem("g_dmask"), 1)

            differences(0)
            stage_read(pool, "zg")
            states_in(0)
            mask_decays(0)
            for s in range(2):
                for l in range(1, LEVELS):
                    if s == 1 and l == 3:
                        pool.wait_ge(sem("gdn_s_stored"), 64)
                        states_in(1)
                    for j in range(2):
                        if l > 1:
                            pool.wait_ge(*full(("dY", s, j, l - 1)))
                        else:
                            pool.wait_ge(sem("g_t0"), 2 * s + j + 1)
                        G.tensor_tensor(g_am[j], g_lt[j], mask4(f"lev{l}", P), ALU.mult).then_inc(sem("g_masked"), 1)
                pool.wait_ge(sem("q_ke"), s + 1)
                link(G.memset(q_kq, 0.0))
                for b in range(DB):
                    G.tensor_copy(q_kq[:, :, 68 * b:68 * b + 4], q_tmp[:, :, 4 * b:4 * b + 4])
                    ins = G.tensor_copy(q_kq[:, :, 68 * b + 32:68 * b + 36], g_q[:, :, SEQ + 4 * b:SEQ + 4 * b + 4])
                ins.then_inc(sem("q_kb"), 1)
                pool.wait_ge(sem("q_dexp"), s + 1)
                G.tensor_tensor(q_dx, q_dx, bc(C("up4", NROW)[:, NS:2 * NS], 1, 4), ALU.mult)
                G.tensor_tensor(q_dy, q_dy, bc(C("low0", NROW)[:, 0:NS], 1, 4), ALU.mult).then_inc(sem("q_dmask"), 1)
                pool.wait_ge(*out(("dchain", s, 3)))
                pool.dma_start(a["gdn_p"][:, 4 * s:4 * s + 4, :], g_s[:, 2, :, :]).then_inc(sem("gdn_p_stored"), 16)
                pool.wait_ge(sem("q_t0"), s + 1)
                G.tensor_tensor(q_am, q_lt, bc(C("lev1", NROW)[:, 0:NS], 1, 4), ALU.mult)
                link(G.tensor_tensor(q_tt, q_lt, bc(C("lev0", NROW)[:, 0:NS], 1, 4), ALU.mult))
                G.tensor_tensor(q_tt, bc(C("ident", NROW)[:, 0:NS], 1, 4), q_tt,
                                ALU.subtract).then_inc(sem("q_masked"), 1)
                pool.wait_ge(*full(("dsX", s)))
                for h in range(4):
                    G.tensor_tensor(g_s0[h], g_s0[h], bc(g_egc[:, h, 4:12], 2, P), ALU.mult
                                    ).then_inc(sem("s0_scaled"), 1)
                if s == 0:
                    pool.wait_ge(*full(("dsO", 0)))
                    differences(1)
                    mask_decays(1)
                for h in range(4):
                    for q in range(2):
                        pool.wait_ge(*out(("dsS", s, h, q)))
                    pool.dma_start(a["gdn_s"][:, 4 * s + h], g_s0[h]).then_inc(sem("gdn_s_stored"), 16)
            pool.wait_ge(sem("gdn_s_stored"), 128)
            pool.wait_ge(sem("gdn_p_stored"), 32)
            low_parts(pool, G, 6, 1, lambda d: g_c[:, 16 + d, :])

        block = ctx.enter_context(nc.Block())
        phases = PHASES

        @block.sync
        def _(sp):
            for st in [s for ph in phases for s in PHASE_STAGES[ph]]:
                kind, n, u0, _ = TABLE[st]
                src, row, w = (a["w2"], W2_ROW[st], UW2) if kind == "down" else (a["w1"], W1_ROW[st], UW1)

                def load(i, j, u0=u0, src=src, row=row, w=w):
                    sp.wait_ge(lo_ready, i * 4 + (u0 + j - RAW + 1))
                    slot = (u0 + j) % RAW
                    sp.dma_start(raw[slot][:, 0:w], src[i * 4 + (row + j)]).then_inc(raw_in[slot], 16)

                if u0 == 0:
                    for j in range(4):
                        sp.dma_start(raw[j][:, 0:w], src[row + j]).then_inc(raw_in[j], 16)
                    with sp.Fori(1, n // 4) as i:
                        for j in range(4):
                            sp.wait_ge(lo_ready, i * 4 + (j - RAW + 1))
                            sp.dma_start(raw[j][:, 0:w], src[i * 4 + (row + j)]).then_inc(raw_in[j], 16)
                else:
                    units(sp, n, load)

            n = int(phases[-1][-1])
            for q in range(2):
                sp.wait_ge(sem("x_new"), DT * n + 4 * q + 4)
                sp.dma_start(a["y"][:, 4 * q:4 * q + 4, :], x[:, 4 * q:4 * q + 4, :]).then_inc(sem("y_stored"), 16)
            sp.wait_ge(sem("y_stored"), 32)

        def width(unit):
            return UW2 if FIRST_UNIT[unit][1] == "down" else UW1

        def last_unit():
            st = [s for ph in phases for s in PHASE_STAGES[ph]][-1]
            return TABLE[st][2] + TABLE[st][1]

        def next_width(u0, kind, i, j):
            if not isinstance(i, int):
                return UW2 if kind == "down" else UW1
            u = u0 + 4 * i + j + 2
            return width(u) if u < last_unit() else 0

        def left_to_norm(name, i, j):
            return name in NORM_STAGE.values() and isinstance(i, int) and 4 * i + j == TABLE[name][1] - 1

        def second_unit(n):
            u = TABLE[NORM_STAGE[n]][2] + TABLE[NORM_STAGE[n]][1] + 1
            return u if u < last_unit() else None

        def split_hi(act, i, c, w):
            act.wait_ge(raw_in[c % RAW], (i + (c // 4 + 1)) * 16)
            if c >= SPL:
                act.wait_ge(unit_done, i * 4 + (c - SPL + 1))
            nc.scalar.activation(whi[c % SPL][:, 0:w], raw[c % RAW][:, 0:w], ACT.Copy).then_inc(hi_ready, 1)

        def split_lo(dve, i, c, w):
            dve.wait_ge(hi_ready, i * 4 + (c + 1))
            nc.vector.tensor_tensor(wlo[c % SPL][:, 0:w], raw[c % RAW][:, 0:w],
                                    whi[c % SPL][:, 0:w].bitcast(F32), ALU.subtract).then_inc(lo_ready, 1)

        @block.tensor
        def _(pe):
            at = [0]

            def start(key):
                assert JOBS[key] == at[0], (key, at[0])
                at[0] += 1
                wait_count(pe, *empty(key))
                return jobb[bank_of(key)]

            def stage(name, version, behind=None):
                kind, n, u0, use = TABLE[name]
                def body(i, j):
                    pe.wait_ge(lo_ready, i * 4 + (u0 + j + 1))
                    s = (u0 + j) % SPL
                    if kind == "down":
                        bank, parts, f0 = gemm[j - j % 2], 11, 11 * (j % 2)
                        hi, lo = hhi, hlo
                    else:
                        bank, parts, f0 = gemm[j], 8, 0
                        hi, lo = xhi, xlo
                    first_unit = isinstance(i, int) and i == 0 and j == 0
                    if kind == "down" and isinstance(i, int) and i == 0 and j < 2:
                        pe.wait_ge(hid_lo, FT * version + 11 * (j + 1))
                    if kind != "down" or j % 2 == 0:
                        wait_count(pe, bank_free[j], i + use[j])
                    for q in range(parts):
                        w = slice(q * P, (q + 1) * P)
                        first = q == 0 and f0 == 0
                        last = q == parts - 1 and (kind != "down" or j % 2 == 1)
                        if first_unit and kind != "down":
                            pe.wait_ge(x_hi, DT * version + q + 1)
                        pe.matmul(bank[:, 0:T], whi[s][:, w], hi[:, f0 + q, :], start=first, stop=False)
                        pe.matmul(bank[:, 0:T], wlo[s][:, w], hi[:, f0 + q, :], start=False, stop=False)
                        if first_unit and kind != "down":
                            pe.wait_ge(x_lo[q % 2], DT // 2 * version + q // 2 + 1)
                        mm = pe.matmul(bank[:, 0:T], whi[s][:, w], lo[:, f0 + q, :], start=False, stop=last)
                    mm.then_inc(unit_done, 1)
                    if behind:
                        behind(4 * i + j)

                units(pe, n, body, peel=True, loop=kind not in WRITTEN_OUT)

            def keep_warm(n):
                if f"norm{n}" == phases[-1]:
                    return
                names = [name for name, _, _ in STAGES]
                bank_use = TABLE[names[names.index(NORM_STAGE[n]) + 1]][3][0]
                wait_count(pe, bank_free[0], bank_use)
                for _ in range(WARM):
                    pe.matmul(gemm[0][:, 0:T], C("mean"), xsum[:], start=True, stop=True)

            def norm(n):
                pe.wait_ge(sem("const_in"), 64)
                bank = start(("mean", n))
                pe.wait_ge(sem("summed"), n + 1)
                pe.matmul(bank[:, 0:T], C("mean"), xsum[:], start=True, stop=False)
                stage_read(pe, NORM_STAGE[n])
                pe.matmul(bank[:, 0:T], C("mean"), r3[:, DT - 1, :], start=False, stop=True
                          ).then_inc(filled[bank_of(("mean", n))], 1)
                bank = start(("var", n))
                for d in range(DT):
                    pe.wait_ge(sem("squared"), DT * n + d + 1)
                    mm = pe.matmul(bank[:, 0:T], C("mean"), x[:, d, :], start=(d == 0), stop=(d == DT - 1))
                mm.then_inc(filled[bank_of(("var", n))], 1)
                keep_warm(n)

            env = dict(start=start, stage=stage)
            for ph in phases:
                kind, n = ph[:-1], int(ph[-1])
                if kind == "ffn":
                    stage(f"up{n}", FFN_VERSION[n])
                    stage(f"down{n}", n)
                elif kind == "norm":
                    norm(n)
                elif kind == "ab":
                    ab_tensor(pe, env)
                elif kind == "gdn":
                    gdn_tensor(pe, env)

        @block.scalar
        def _(act):
            chain = [0]

            def link(ins):
                chain[0] += 1
                ins.then_inc(sem("act_chain"), 1)
                act.wait_ge(sem("act_chain"), chain[0])

            def stage(name, consume):
                kind, n, u0, use = TABLE[name]

                def body(i, j):
                    w = next_width(u0, kind, i, j)
                    if kind not in SPLIT_FIRST:
                        consume(i, j, u0, use)
                    if w and not left_to_norm(name, i, j):
                        split_hi(act, i, u0 + j + 2, w)
                    if kind in SPLIT_FIRST:
                        consume(i, j, u0, use)

                units(act, n, body, peel=u0 == 0 or kind in SPLIT_FIRST, loop=kind not in WRITTEN_OUT)

            def silu(i, j, u0, use):
                if j % 2 == 0:
                    act.wait_ge(unit_done, i * 4 + (u0 + j + 1))
                    if j == 0 or j == 2:
                        wait_count(act, bank_free[j + 1], i + use[j + 1])
                    nc.scalar.activation(sg[:, j // 2, :], gemm[j][:, 0:T], ACT.Silu).then_inc(bank_free[j], 1)

            def idle(i, j, u0, use):
                pass

            def preload(func):
                nc.scalar.activation(act_scratch[:, 0:1], act_scratch[:, 1:2], func)

            def norm(n):
                if n == 0:
                    act.wait_ge(sem("const_in"), 64)
                preload(ACT.Sqrt)
                for d in range(DT):
                    if d < DT - 1:
                        act.wait_ge(sem("centred"), (DT - 1) * n + d + 1)
                    else:
                        act.wait_ge(*out(("mean", n)))
                    nc.scalar.activation(x[:, d, :], r3[:, d, :], ACT.Square).then_inc(sem("squared"), 1)
                if second_unit(n):
                    split_hi(act, 0, second_unit(n), width(second_unit(n)))
                act.wait_ge(*full(("var", n)))
                eps = C("eps")[:, (0 if n in (1, 4) else 1):][:, 0:1]
                nc.scalar.activation(m(0, T), jobb[bank_of(("var", n))][:, 0:T], ACT.Sqrt,
                                     bias=eps).then_inc(drained[bank_of(("var", n))], 1)
                for d in range(DT):
                    act.wait_ge(sem("scaled"), DT * n + d + 1)
                    b = pc("ln_b", n * DT + d)
                    if f"norm{n}" != phases[-1]:
                        nc.scalar.activation(xhi[:, d, :], r3[:, d, :], ACT.Identity, bias=b).then_inc(x_hi, 1)
                    else:
                        nc.scalar.activation(x[:, d, :], r3[:, d, :], ACT.Identity, bias=b).then_inc(sem("x_new"), 1)
                if f"norm{n}" != phases[-1]:
                    for d in range(DT):
                        nc.scalar.activation(x[:, d, :], r3[:, d, :], ACT.Identity, bias=pc("ln_b", n * DT + d)
                                             ).then_inc(sem("x_new"), 1)

            for q in range(2):
                act.dma_start(x[:, 4 * q:4 * q + 4, :], a["x"][:, 4 * q:4 * q + 4, :]).then_inc(sem(f"x_in{q}"), 16)
            for q in range(2):
                split_hi(act, 0, q, UW1)
                act.wait_ge(sem(f"x_in{q}"), 16)
                for d in range(4 * q, 4 * q + 4):
                    nc.scalar.activation(xhi[:, d, :], x[:, d, :], ACT.Copy).then_inc(x_hi, 1)
            act.wait_ge(sem("scratch_set"), 1)
            env = dict(link=link, stage=stage, idle=idle)
            for ph in phases:
                kind, n = ph[:-1], int(ph[-1])
                if kind == "ffn":
                    preload(ACT.Silu)
                    stage(f"up{n}", silu)
                    stage(f"down{n}", idle)
                elif kind == "norm":
                    norm(n)
                elif kind == "ab":
                    ab_scalar(act, env)
                elif kind == "gdn":
                    gdn_scalar(act, env)

        @block.vector
        def _(dve):
            chain = [0]

            def link(ins):
                chain[0] += 1
                ins.then_inc(sem("dve_chain"), 1)
                dve.wait_ge(sem("dve_chain"), chain[0])

            def stage(name, consume):
                kind, n, u0, use = TABLE[name]

                def body(i, j):
                    w = next_width(u0, kind, i, j)
                    if kind not in SPLIT_FIRST:
                        consume(i, j, u0, use)
                    if w and not left_to_norm(name, i, j):
                        split_lo(dve, i, u0 + j + 2, w)
                    if kind in SPLIT_FIRST:
                        consume(i, j, u0, use)

                units(dve, n, body, peel=u0 == 0 or kind in SPLIT_FIRST, loop=kind not in WRITTEN_OUT)

            def gated(ffn):
                def consume(i, j, u0, use):
                    if j % 2 == 1:
                        h = j // 2
                        dve.wait_ge(unit_done, i * 4 + (u0 + j + 1))
                        dve.wait_ge(bank_free[j - 1], i + (use[j - 1] + 1))
                        wait_count(dve, hid_lo, i * 2 + FT * ffn)
                        nc.vector.tensor_tensor(hb[:, h, :], sg[:, h, :], gemm[j][:, 0:T],
                                                ALU.mult).then_inc(bank_free[j], 1)
                return consume

            def residual(scale, kind):
                def consume(i, j, u0, use):
                    if kind == "down":
                        if j % 2 == 0:
                            return
                        bank, d = j - 1, i * 2 + j // 2
                    else:
                        bank, d = j, i * 4 + j
                    dve.wait_ge(unit_done, i * 4 + (u0 + j + 1))
                    nc.vector.scalar_tensor_tensor(out=r3[:, d, :], in0=x[:, d, :], scalar=scale,
                                                   in1=gemm[bank][:, 0:T], op0=ALU.mult,
                                                   op1=ALU.add).then_inc(bank_free[bank], 1)
                return consume

            def norm(n, stage_name):
                if n == 0:
                    dve.wait_ge(sem("const_in"), 64)
                stage_read(dve, stage_name)
                dve.wait_ge(*full(("mean", n)))
                for d in range(DT):
                    ins = nc.vector.tensor_tensor(r3[:, d, :], r3[:, d, :], jobb[bank_of(("mean", n))][:, 0:T],
                                                  ALU.subtract)
                    if d < DT - 1:
                        ins.then_inc(sem("centred"), 1)
                    else:
                        ins.then_inc(drained[bank_of(("mean", n))], 1)
                if second_unit(n):
                    split_lo(dve, 0, second_unit(n), width(second_unit(n)))
                dve.wait_ge(*out(("var", n)))
                link(nc.vector.reciprocal(m(T, T), m(0, T)))
                for d in range(DT):
                    nc.vector.scalar_tensor_tensor(out=r3[:, d, :], in0=r3[:, d, :], scalar=pc("ln_g", n * DT + d),
                                                   in1=m(T, T), op0=ALU.mult, op1=ALU.mult
                                                   ).then_inc(sem("scaled"), 1)
                if f"norm{n}" != phases[-1]:
                    for d in range(DT):
                        dve.wait_ge(x_hi, DT * X_VERSION[n] + d + 1)
                        nc.vector.scalar_tensor_tensor(out=xlo[:, d, :], in0=r3[:, d, :],
                                                       scalar=pc("ln_b", n * DT + d),
                                                       in1=xhi[:, d, :].bitcast(F32), op0=ALU.add,
                                                       op1=ALU.subtract).then_inc(x_lo[d % 2], 1)

            for q in range(2):
                split_lo(dve, 0, q, UW1)
                dve.wait_ge(sem(f"x_in{q}"), 16)
                for d in (4 * q, 4 * q + 2):
                    dve.wait_ge(x_hi, d + 1)
                    nc.vector.tensor_tensor(xlo[:, d, :], x[:, d, :], xhi[:, d, :].bitcast(F32), ALU.subtract
                                            ).then_inc(x_lo[0], 1)
            env = dict(link=link, stage=stage, residual=residual)
            for ph in phases:
                kind, n = ph[:-1], int(ph[-1])
                if kind == "ffn":
                    stage(f"up{n}", gated(n))
                    stage(f"down{n}", residual(2.0 * ALPHA, "down"))
                elif kind == "norm":
                    norm(n, NORM_STAGE[n])
                elif kind == "ab":
                    ab_vector(dve, env)
                elif kind == "gdn":
                    gdn_vector(dve, env)

        @block.gpsimd
        def _(pool):
            nc.gpsimd.memset(act_scratch[:], 1.0).then_inc(sem("scratch_set"), 1)
            chain = [0]

            def link(ins):
                chain[0] += 1
                ins.then_inc(sem("pool_chain"), 1)
                pool.wait_ge(sem("pool_chain"), chain[0])

            def sum_tiles(n):
                kind, _, _, use = TABLE[NORM_STAGE[n]]
                for d in range(DT - 1):
                    bank = 2 * (d % 2) if kind == "down" else d % 4
                    pool.wait_ge(bank_free[bank], use[bank] + (d // 2 if kind == "down" else d // 4) + 1)
                    if d == 0:
                        continue
                    ins = nc.gpsimd.tensor_tensor(xsum[:], r3[:, 0, :] if d == 1 else xsum[:], r3[:, d, :], ALU.add)
                    if d < DT - 2:
                        link(ins)
                ins.then_inc(sem("summed"), 1)

            def split_hidden(ffn):
                use = TABLE[f"up{ffn}"][3]

                def tile(i, h):
                    f = i * 2 + h
                    pool.wait_ge(bank_free[2 * h + 1], i + (use[2 * h + 1] + 1))
                    nc.gpsimd.tensor_copy(hhi[:, f, :], hb[:, h, :]).then_inc(hid_hi, 1)
                    pool.wait_ge(hid_hi, f + (FT * ffn + 1))
                    nc.gpsimd.tensor_tensor(hlo[:, f, :], hb[:, h, :], hhi[:, f, :].bitcast(F32),
                                            ALU.subtract).then_inc(hid_lo, 1)

                with pool.Fori(0, FT // 2) as i:
                    tile(i, 0)
                    tile(i, 1)

            env = dict(link=link)
            low_parts(pool, nc.gpsimd, 0, 1, lambda d: x[:, d, :])
            pool.dma_start(cst[:], a["const"]).then_inc(sem("const_in"), 16)
            pool.dma_start(mixc[:, 0:CONST_AB.shape[1]], a["const_ab"]).then_inc(sem("const_in"), 16)
            pool.dma_start(par[:], a["par"]).then_inc(sem("const_in"), 16)
            pool.dma_start(g2w2, a["lora"]).then_inc(sem("const_in"), 16)
            for ph in phases:
                kind, n = ph[:-1], int(ph[-1])
                if kind == "ffn":
                    split_hidden(n)
                elif kind == "norm":
                    sum_tiles(n)
                    if n == 1:
                        pool.wait_ge(sem("stored"), 80)
                    if n == 1 and "gdn0" in phases:
                        pool.dma_start(mixc[:, 0:CONST_GD.shape[1]], a["const_gd"]).then_inc(sem("const_gd_in"), 16)
                elif kind == "ab":
                    ab_pool(pool, env)
                elif kind == "gdn":
                    gdn_pool(pool, env)
            pool.wait_ge(sem("stored"), 80)
            if "gdn0" in phases:
                pool.wait_ge(sem("conv_stored"), 16)
                pool.wait_ge(sem("gdn_p_stored"), 32)
                pool.wait_ge(sem("gdn_s_stored"), 128)


def _tiles(v):
    return v.reshape(-1, P).T


def _w1(w):
    k, n = w.shape
    return w.reshape(k // P, P, n // P, P).transpose(2, 1, 0, 3).reshape(n // P, P, (k // P) * P)


def lay_out(i):
    f = np.float32
    x = np.concatenate([i["x_prompt"].reshape(SEQ, D), i["x_sample"].reshape(NS, D)], 0)
    a = {"x": x.reshape(T, DT, P).transpose(2, 1, 0)}
    w1, w2 = [], []
    for name, kind, n in STAGES:
        if kind == "up":
            f_ = int(name[2:])
            g, u = (_w1(i[k][f_ // 2, f_ % 2]) for k in ("ffn_w_gate", "ffn_w_up"))
            w1.append(np.stack([g, u], 1).reshape(n, P, UW1))
        elif kind == "down":
            f_ = int(name[4:])
            w = _w1(i["ffn_w_down"][f_ // 2, f_ % 2])
            w2.append(w.reshape(DT, P, 2, UW2).transpose(0, 2, 1, 3).reshape(n, P, UW2))
        elif name == "za":
            w1.append(_w1(i["ab_w_in"][0][:, :ZA * P])[ZA_ORDER])
        elif name == "zb":
            w1.append(_w1(i["ab_w_in"][0][:, ZA * P:]))
        elif name == "abo":
            w1.append(_w1(i["ab_w_out"][0]))
        elif name == "qk":
            w1.append(_w1(i["gdn_w_in"][0][:, :16 * P]))
        elif name == "v":
            w1.append(_w1(i["gdn_w_in"][0][:, 16 * P:QKV * P]))
        elif name == "ba":
            w = np.zeros((D, P), f)
            w[:, 0:HC] = i["gdn_w_in"][0][:, QKV * P:QKV * P + HC]
            w[:, 32:32 + HC] = i["gdn_w_in"][0][:, QKV * P + HC:QKV * P + 2 * HC]
            w1.append(_w1(w))
        elif name == "zg":
            w1.append(_w1(i["gdn_w_in"][0][:, QKV * P + 2 * HC:]))
        elif name == "gdo":
            w1.append(_w1(i["gdn_w_out"][0]))
    a["w1"], a["w2"] = np.concatenate(w1, 0), np.concatenate(w2, 0)
    par = np.zeros((P, NPAR), f)

    def put(name, v, rows=slice(0, P)):
        at, w = PCOLS[name]
        par[rows, at:at + w] = v

    put("ln_g", _tiles(i["ln_g"].reshape(-1)))
    put("ln_b", _tiles(i["ln_b"].reshape(-1)))
    for name, key in (("mu", "rwkv_mu"), ("w0", "rwkv_w0"), ("a0", "rwkv_a0"), ("kk", "rwkv_k_k"), ("ka", "rwkv_k_a"),
                      ("rk", "rwkv_r_k"), ("gng", "rwkv_gn_g"), ("gnb", "rwkv_gn_b"), ("rgg", "ret_gn_g"),
                      ("rgb", "ret_gn_b")):
        put(name, _tiles(i[key][0].reshape(-1)))
    put("conv", _tiles(i["gdn_conv_w"][0].reshape(-1)))
    put("ng", i["gdn_norm_g"][0].reshape(P, 1))
    put("alog", i["gdn_A_log"][0].reshape(HC, 1), slice(32, 32 + HC))
    put("dtb", i["gdn_dt_bias"][0].reshape(HC, 1), slice(32, 32 + HC))
    a["par"] = par
    a["lora"] = np.concatenate([np.concatenate([i["rwkv_w2"][0], i["rwkv_a2"][0]], 0), i["rwkv_g2"][0]], 1)
    a["const"], a["const_ab"], a["const_gd"] = CONST_ALL, CONST_AB, CONST_GD
    a["shift_in"] = i["state_rwkv_shift"][0].reshape(DB, ZA, P).transpose(2, 1, 0)
    a["rwkv_in"] = i["state_rwkv"][0].reshape(DB, 4, 2, 64, 64).transpose(2, 4, 1, 0, 3).reshape(P, 4, DB, 64)
    a["ret_in"] = i["state_ret"][0].transpose(2, 1, 0, 3)
    a["conv_in"] = i["state_gdn_conv"][0].reshape(DB, 3, QKV, P).transpose(3, 2, 0, 1)
    a["gdn_in"] = i["state_gdn"][0].transpose(2, 1, 0, 3)
    return {k: np.ascontiguousarray(v) for k, v in a.items()}


OUTS = {"y": (P, DT, T), "shift_out": (P, ZA, 9), "rwkv_p": (P, 4, 64), "rwkv_s": (P, 4, DB, 64),
        "ret_p": (P, HB, P), "ret_s": (P, HB, DB, P), "conv_out": (P, QKV, 27), "gdn_p": (P, HC, P),
        "gdn_s": (P, HC, DB, P)}


def unpack(o):
    y = o["y"].transpose(2, 1, 0).reshape(T, D)
    sh = o["shift_out"].transpose(2, 1, 0).reshape(9, ZA * P)
    rp = o["rwkv_p"].reshape(2, 64, 4, 64).transpose(2, 0, 3, 1).reshape(1, 1, HA, 64, 64)
    rs = o["rwkv_s"].reshape(2, 64, 4, DB, 64).transpose(3, 2, 0, 4, 1).reshape(1, DB, HA, 64, 64)
    cv = o["conv_out"].transpose(2, 1, 0).reshape(27, QKV * P)
    return tuple(np.ascontiguousarray(v) for v in (
        y[:SEQ].reshape(1, SEQ, D), y[SEQ:].reshape(DB, DS, D), sh[0:1][None], rp,
        o["ret_p"].transpose(1, 0, 2)[None, None], cv[0:3][None, None], o["gdn_p"].transpose(1, 0, 2)[None, None],
        sh[1:][None], rs, o["ret_s"].transpose(2, 1, 0, 3)[None], cv[3:].reshape(1, DB, 3, QKV * P),
        o["gdn_s"].transpose(2, 1, 0, 3)[None]))


def declare(nc, arrays):
    aps = {k: nc.dram_tensor(f"in_{k}_dram", v.shape, mybir.dt.from_np(v.dtype), kind="ExternalInput").ap()
           for k, v in arrays.items()}
    for k, shape in OUTS.items():
        aps[k] = nc.dram_tensor(f"out_{k}_dram", shape, F32, kind="ExternalOutput").ap()
    return aps


def kernel(**inputs):
    import concourse.bacc as _bacc
    from concourse.bass_utils import run_bass_kernel_spmd as _run

    arrays = lay_out({k: np.asarray(v) for k, v in inputs.items()})
    nc = _bacc.Bacc("TRN2", target_bir_lowering=False, num_devices=1)
    delta_kernel(nc, declare(nc, arrays))
    r = _run(nc, [{f"in_{k}_dram": v for k, v in arrays.items()}], core_ids=[0])
    return unpack({k: r.results[0][f"out_{k}_dram"] for k in OUTS})
```
